# Optimizing a Trainium2 kernel written in Bass

```python
import math, functools
import jax, jax.numpy as jnp
from jax import lax
import numpy as np

D_MODEL = 1024
BATCH = 1
SEQ = 512
DEPTH = 1

HEAD_DIM = 64
N_META = 16
BLOCK_Q = 128
PAD = BLOCK_Q - N_META
SEG_BLOCKS = 8
SUB = 64
RWKV_HEADS = 6
SB_HEADS = 5
FOX_HEADS = 5
RWKV_W = RWKV_HEADS * HEAD_DIM
SB_W = SB_HEADS * HEAD_DIM
FOX_W = FOX_HEADS * HEAD_DIM
DECAY_RANK = 64
ICLR_RANK = 64
N_BRANCH = 3
SHIFT_W = 3 * RWKV_W + DECAY_RANK + ICLR_RANK
REST_W = 3 * SB_W + 3 * FOX_W + FOX_HEADS + N_BRANCH * D_MODEL
D_IN = SHIFT_W + REST_W
N_GROUPS = 4
EXPERTS_PER_GROUP = 4
N_EXPERTS = N_GROUPS * EXPERTS_PER_GROUP
TOP_K = 2
D_EXPERT = 256
NORM_EPS = 1e-6
RWKV_LN_EPS = 64e-5
NEG_INF = -1e30

kernel_name = "hybrid_rwkv7_stickbreak_fox_hiermoe"

def rms_norm(x, g, eps=NORM_EPS):
    xf = x.astype(jnp.float32)
    y = xf * lax.rsqrt(jnp.mean(xf * xf, axis=-1, keepdims=True) + eps)
    return (y * g.astype(jnp.float32)).astype(x.dtype)

def token_shift(u, mu):
    prev = jnp.pad(u, ((0, 0), (1, 0), (0, 0)))[:, :-1]
    return u + (prev - u) * mu

def rwkv7_time_mix(r, k, v, wd, ad, w_up, w0, a_up, a0, k_k, k_a, r_k, ln_g, ln_b):
    dt = r.dtype
    f32 = jnp.float32
    B, L, _ = r.shape
    logw = -jax.nn.softplus(-(w0 + jnp.tanh(wd) @ w_up).astype(f32)) - 0.5
    decay = jnp.exp(-jnp.exp(logw))
    a = jax.nn.sigmoid((a0 + ad @ a_up).astype(f32))
    hs = lambda u: u.astype(f32).reshape(B, L, RWKV_HEADS, HEAD_DIM)
    r, k, v, decay, a = hs(r), hs(k), hs(v), hs(decay), hs(a)
    kk = k * k_k.astype(f32)
    kk = kk / jnp.maximum(jnp.sqrt(jnp.sum(kk * kk, axis=-1, keepdims=True)), 1e-12)
    k = k * (1.0 + (a - 1.0) * k_a.astype(f32))

    def step(S, inp):
        r_t, w_t, k_t, v_t, kk_t, a_t = inp
        sa = jnp.einsum('bhvk,bhk->bhv', S, -kk_t)
        S = (S * w_t[:, :, None, :]
             + sa[..., None] * (kk_t * a_t)[:, :, None, :]
             + v_t[..., None] * k_t[:, :, None, :])
        return S, jnp.einsum('bhvk,bhk->bhv', S, r_t)

    xs = (jnp.moveaxis(r, 1, 0), jnp.moveaxis(decay, 1, 0), jnp.moveaxis(k, 1, 0),
          jnp.moveaxis(v, 1, 0), jnp.moveaxis(kk, 1, 0), jnp.moveaxis(a, 1, 0))
    S0 = jnp.zeros((B, RWKV_HEADS, HEAD_DIM, HEAD_DIM), f32)
    _, y = lax.scan(step, S0, xs)
    y = jnp.moveaxis(y, 0, 1)
    mean = jnp.mean(y, axis=-1, keepdims=True)
    var = jnp.mean(jnp.square(y - mean), axis=-1, keepdims=True)
    y = (y - mean) * lax.rsqrt(var + RWKV_LN_EPS)
    y = y.reshape(B, L, RWKV_W) * ln_g.astype(f32) + ln_b.astype(f32)
    bonus = jnp.sum(r * k * r_k.astype(f32), axis=-1, keepdims=True) * v
    return (y + bonus.reshape(B, L, RWKV_W)).astype(dt)

def to_padded_heads(u, n_heads):
    B, L, _ = u.shape
    u = u.reshape(B, L, n_heads, HEAD_DIM).transpose(0, 2, 1, 3)
    return jnp.pad(u, ((0, 0), (0, 0), (PAD, 0), (0, 0)))

def from_padded_heads(o):
    B, H, T, d = o.shape
    return o[:, :, PAD:].transpose(0, 2, 1, 3).reshape(B, T - PAD, H * d)

def causal_sweep(block_fn, n_blocks):
    outs = []
    for b0 in range(0, n_blocks, SEG_BLOCKS):
        b1 = min(b0 + SEG_BLOCKS, n_blocks)
        outs.append(lax.map(functools.partial(block_fn, key_len=b1 * BLOCK_Q), jnp.arange(b0, b1)))
    return jnp.concatenate(outs, axis=0)

def stick_breaking_attention(q, k, v):
    B, H, T, d = q.shape
    scale = 1.0 / math.sqrt(d)
    f32 = jnp.float32

    def block(i, key_len):
        nsub = key_len // SUB
        kb, vb = k[:, :, :key_len], v[:, :, :key_len]
        q0 = i * BLOCK_Q
        qb = lax.dynamic_slice_in_dim(q, q0, BLOCK_Q, axis=2)
        z = jnp.einsum('bhqd,bhkd->bhqk', qb, kb, preferred_element_type=f32) * scale
        key_pos = jnp.arange(key_len)
        qpos = q0 + jnp.arange(BLOCK_Q)
        mask = (key_pos[None, :] < qpos[:, None]) & (key_pos[None, :] >= PAD)
        log_1mb = jnp.where(mask, jax.nn.log_sigmoid(-z), 0.0)
        lr = log_1mb.reshape(B, H, BLOCK_Q, nsub, SUB)
        j_in = jnp.arange(SUB)
        upper_in = (j_in[:, None] > j_in[None, :]).astype(f32)
        tail_in = jnp.einsum('bhqnj,js->bhqns', lr, upper_in)
        m_blk = jnp.arange(nsub)
        upper_blk = (m_blk[:, None] > m_blk[None, :]).astype(f32)
        later = jnp.einsum('bhqm,mn->bhqn', jnp.sum(lr, axis=-1), upper_blk)
        tail = (tail_in + later[..., None]).reshape(B, H, BLOCK_Q, key_len)
        A = jnp.where(mask, jnp.exp(jax.nn.log_sigmoid(z) + tail), 0.0)
        return jnp.einsum('bhqk,bhkd->bhqd', A.astype(v.dtype), vb)

    out = causal_sweep(block, T // BLOCK_Q)
    return out.transpose(1, 2, 0, 3, 4).reshape(B, H, T, d)

def forgetting_attention(q, k, v, logf_cum):
    B, H, T, d = q.shape
    scale = 1.0 / math.sqrt(d)

    def block(i, key_len):
        kb, vb, fk = k[:, :, :key_len], v[:, :, :key_len], logf_cum[:, :, :key_len]
        q0 = i * BLOCK_Q
        qb = lax.dynamic_slice_in_dim(q, q0, BLOCK_Q, axis=2)
        fq = lax.dynamic_slice_in_dim(logf_cum, q0, BLOCK_Q, axis=2)
        s = jnp.einsum('bhqd,bhkd->bhqk', qb, kb, preferred_element_type=jnp.float32) * scale
        s = s + fq[..., :, None] - fk[:, :, None, :]
        key_pos = jnp.arange(key_len)
        qpos = q0 + jnp.arange(BLOCK_Q)
        mask = (key_pos[None, :] <= qpos[:, None]) & (key_pos[None, :] >= PAD)
        p = jax.nn.softmax(jnp.where(mask, s, NEG_INF), axis=-1)
        return jnp.einsum('bhqk,bhkd->bhqd', p.astype(v.dtype), vb)

    out = causal_sweep(block, T // BLOCK_Q)
    return out.transpose(1, 2, 0, 3, 4).reshape(B, H, T, d)

def hybrid_mixer(n, w_in, rwkv_mu, rwkv_w_up, rwkv_w0, rwkv_a_up, rwkv_a0, rwkv_k_k, rwkv_k_a,
                 rwkv_r_k, rwkv_ln_g, rwkv_ln_b, fox_f_b, fox_q_g, fox_k_g,
                 w_p_rwkv, w_p_sb, w_p_fox, w_out):
    B, L, D = n.shape
    u = n @ w_in
    u_shift = token_shift(u[..., :SHIFT_W], rwkv_mu)
    u_rest = u[..., SHIFT_W:]
    r, k, v, wd, ad = jnp.split(
        u_shift, [RWKV_W, 2 * RWKV_W, 3 * RWKV_W, 3 * RWKV_W + DECAY_RANK], axis=-1)
    sbq, sbk, sbv, fq, fk, fv, f_logit, gates = jnp.split(
        u_rest, [SB_W, 2 * SB_W, 3 * SB_W, 3 * SB_W + FOX_W, 3 * SB_W + 2 * FOX_W,
                 3 * SB_W + 3 * FOX_W, 3 * SB_W + 3 * FOX_W + FOX_HEADS], axis=-1)

    y_a = rwkv7_time_mix(r, k, v, wd, ad, rwkv_w_up, rwkv_w0, rwkv_a_up, rwkv_a0,
                         rwkv_k_k, rwkv_k_a, rwkv_r_k, rwkv_ln_g, rwkv_ln_b)

    y_b = from_padded_heads(stick_breaking_attention(
        to_padded_heads(sbq, SB_HEADS), to_padded_heads(sbk, SB_HEADS), to_padded_heads(sbv, SB_HEADS)))

    fq = rms_norm(fq.reshape(B, L, FOX_HEADS, HEAD_DIM), fox_q_g).reshape(B, L, FOX_W)
    fk = rms_norm(fk.reshape(B, L, FOX_HEADS, HEAD_DIM), fox_k_g).reshape(B, L, FOX_W)
    logf = jax.nn.log_sigmoid((f_logit + fox_f_b).astype(jnp.float32))
    logf = jnp.pad(logf, ((0, 0), (PAD, 0), (0, 0)))
    logf_cum = jnp.cumsum(logf, axis=1).transpose(0, 2, 1)
    y_c = from_padded_heads(forgetting_attention(
        to_padded_heads(fq, FOX_HEADS), to_padded_heads(fk, FOX_HEADS),
        to_padded_heads(fv, FOX_HEADS), logf_cum))

    g = jax.nn.sigmoid(gates).reshape(B, L, N_BRANCH, D)
    merged = (g[:, :, 0] * (y_a @ w_p_rwkv)
              + g[:, :, 1] * (y_b @ w_p_sb)
              + g[:, :, 2] * (y_c @ w_p_fox))
    return merged @ w_out

def hierarchical_moe(n, wg, bg, we, be, w_gate, w_up, w_down):
    B, L, D = n.shape
    t = n.reshape(B * L, D)
    N = t.shape[0]
    lg = (t @ wg + bg).astype(jnp.float32)
    pg = jax.nn.softmax(lg, axis=-1)
    g_idx = jnp.argmax(lg, axis=-1)
    p_group = jnp.take_along_axis(pg, g_idx[:, None], axis=-1)
    le = (t @ we + be).astype(jnp.float32).reshape(N, N_GROUPS, EXPERTS_PER_GROUP)
    le_sel = jnp.take_along_axis(le, g_idx[:, None, None], axis=1)[:, 0]
    top_v, top_i = lax.top_k(le_sel, TOP_K)
    p_top = jax.nn.softmax(top_v, axis=-1)
    expert_id = g_idx[:, None] * EXPERTS_PER_GROUP + top_i
    combine = jnp.sum(jax.nn.one_hot(expert_id, N_EXPERTS, dtype=jnp.float32)
                      * (p_group * p_top)[..., None], axis=1).astype(t.dtype)
    y = jnp.zeros_like(t)
    for e in range(N_EXPERTS):
        he = jax.nn.silu(t @ w_gate[e]) * (t @ w_up[e])
        y = y + combine[:, e:e + 1] * (he @ w_down[e])
    return y.reshape(B, L, D)

def setup_inputs(seed: int = 0) -> dict:
    key = jax.random.key(seed)
    ks = jax.random.split(key, 32)
    f32 = jnp.float32
    nrm = lambda k, shape, s: jax.random.normal(k, shape, f32) * s
    unif = lambda k, shape, lo, hi: jax.random.uniform(k, shape, f32, lo, hi)
    return {
        "x": nrm(ks[0], (BATCH, SEQ, D_MODEL), 1.0),
        "meta_tokens": nrm(ks[1], (N_META, D_MODEL), 1.0),
        "norm1_g": 1.0 + nrm(ks[2], (DEPTH, D_MODEL), 0.02),
        "w_in": nrm(ks[3], (DEPTH, D_MODEL, D_IN), D_MODEL ** -0.5),
        "rwkv_mu": unif(ks[4], (DEPTH, SHIFT_W), 0.0, 1.0),
        "rwkv_w_up": nrm(ks[5], (DEPTH, DECAY_RANK, RWKV_W), 0.1),
        "rwkv_w0": unif(ks[6], (DEPTH, RWKV_W), -6.0, 1.0),
        "rwkv_a_up": nrm(ks[7], (DEPTH, ICLR_RANK, RWKV_W), 0.1),
        "rwkv_a0": nrm(ks[8], (DEPTH, RWKV_W), 0.5),
        "rwkv_k_k": 0.85 + nrm(ks[9], (DEPTH, RWKV_HEADS, HEAD_DIM), 0.05),
        "rwkv_k_a": 1.0 + nrm(ks[10], (DEPTH, RWKV_HEADS, HEAD_DIM), 0.05),
        "rwkv_r_k": nrm(ks[11], (DEPTH, RWKV_HEADS, HEAD_DIM), 0.1),
        "rwkv_ln_g": 1.0 + nrm(ks[12], (DEPTH, RWKV_W), 0.02),
        "rwkv_ln_b": nrm(ks[13], (DEPTH, RWKV_W), 0.02),
        "fox_f_b": unif(ks[14], (DEPTH, FOX_HEADS), 2.0, 6.0),
        "fox_q_g": 1.0 + nrm(ks[15], (DEPTH, HEAD_DIM), 0.02),
        "fox_k_g": 1.0 + nrm(ks[16], (DEPTH, HEAD_DIM), 0.02),
        "w_p_rwkv": nrm(ks[17], (DEPTH, RWKV_W, D_MODEL), RWKV_W ** -0.5),
        "w_p_sb": nrm(ks[18], (DEPTH, SB_W, D_MODEL), SB_W ** -0.5),
        "w_p_fox": nrm(ks[19], (DEPTH, FOX_W, D_MODEL), FOX_W ** -0.5),
        "w_out": nrm(ks[20], (DEPTH, D_MODEL, D_MODEL), D_MODEL ** -0.5),
        "norm2_g": 1.0 + nrm(ks[21], (DEPTH, D_MODEL), 0.02),
        "moe_wg": nrm(ks[22], (DEPTH, D_MODEL, N_GROUPS), D_MODEL ** -0.5),
        "moe_bg": nrm(ks[23], (DEPTH, N_GROUPS), 0.01),
        "moe_we": nrm(ks[24], (DEPTH, D_MODEL, N_EXPERTS), D_MODEL ** -0.5),
        "moe_be": nrm(ks[25], (DEPTH, N_EXPERTS), 0.01),
        "moe_w_gate": nrm(ks[26], (DEPTH, N_EXPERTS, D_MODEL, D_EXPERT), D_MODEL ** -0.5),
        "moe_w_up": nrm(ks[27], (DEPTH, N_EXPERTS, D_MODEL, D_EXPERT), D_MODEL ** -0.5),
        "moe_w_down": nrm(ks[28], (DEPTH, N_EXPERTS, D_EXPERT, D_MODEL), D_EXPERT ** -0.5),
    }

def reference(x, meta_tokens, norm1_g, w_in, rwkv_mu, rwkv_w_up, rwkv_w0, rwkv_a_up, rwkv_a0,
              rwkv_k_k, rwkv_k_a, rwkv_r_k, rwkv_ln_g, rwkv_ln_b, fox_f_b, fox_q_g, fox_k_g,
              w_p_rwkv, w_p_sb, w_p_fox, w_out, norm2_g, moe_wg, moe_bg, moe_we, moe_be,
              moe_w_gate, moe_w_up, moe_w_down):
    B = x.shape[0]
    meta = jnp.broadcast_to(meta_tokens[None].astype(x.dtype), (B, N_META, D_MODEL))
    h = jnp.concatenate([meta, x], axis=1)
    for l in range(DEPTH):
        h = h + hybrid_mixer(rms_norm(h, norm1_g[l]), w_in[l], rwkv_mu[l], rwkv_w_up[l],
                             rwkv_w0[l], rwkv_a_up[l], rwkv_a0[l], rwkv_k_k[l], rwkv_k_a[l],
                             rwkv_r_k[l], rwkv_ln_g[l], rwkv_ln_b[l], fox_f_b[l], fox_q_g[l],
                             fox_k_g[l], w_p_rwkv[l], w_p_sb[l], w_p_fox[l], w_out[l])
        h = h + hierarchical_moe(rms_norm(h, norm2_g[l]), moe_wg[l], moe_bg[l], moe_we[l],
                                 moe_be[l], moe_w_gate[l], moe_w_up[l], moe_w_down[l])
    return h[:, N_META:]


_drawn_inputs = setup_inputs


def setup_inputs(seed=0):
    import zlib

    import numpy as np

    out = dict(_drawn_inputs(seed))
    spreads = {}
    factors = {'rwkv_ln_g': 11.899,
     'rwkv_ln_b': 5.44,
     'fox_q_g': 8.0,
     'fox_k_g': 7.53,
     'moe_bg': 32.246,
     'moe_be': 23.641,
     'norm2_g': 4.523}
    for name, (base, spread) in spreads.items():
        noise = np.random.default_rng([zlib.crc32(name.encode()), seed]).standard_normal(out[name].shape)
        drawn = base * np.exp(spread * noise) if base else spread * noise
        out[name] = __import__('jax').numpy.asarray(drawn.astype(out[name].dtype))
    for name, factor in factors.items():
        out[name] = (out[name] * factor).astype(out[name].dtype)
    return out
```

```python
from contextlib import ExitStack

import concourse.bass as bass
from concourse import mybir

F32 = mybir.dt.float32
U32 = mybir.dt.uint32
I32 = mybir.dt.int32
ALU = mybir.AluOpType
ACT = mybir.ActivationFunctionType
AX = mybir.AxisListType.X

P = 128
D = 1024
DC = D // P
META = 16
SEQ = 512
L = META + SEQ
HALF = L // 2
NT = SEQ // P
HD = 64
RH, SH, FH = 6, 5, 5
RW, SW, FW = RH * HD, SH * HD, FH * HD
RC = RW // P
SHIFT_W = 3 * RW + 2 * HD
SC = SHIFT_W // P
C_SBQ = SHIFT_W
C_SBK = C_SBQ + SW
C_SBV = C_SBK + SW
C_FQ = C_SBV + SW
C_FK = C_FQ + FW
C_FV = C_FK + FW
C_F = C_FV + FW
C_G = C_F + FH
PIECE = 256
RING = 4
RING_W = FW + FH
CH = 64
NCH = -(-L // CH)
LP = NCH * CH
NG, EPG = 4, 4
NE = NG * EPG
DE = 256
EPS = 1e-6
LN_EPS = 64e-5
DECAY = 0.6065306597126334
NEG = -1e30
NOV = SEQ * 2 // P - 1
KT = [(128 * i, min(128, L - 128 * i)) for i in range(5)]


def hybrid_layer(nc, x, meta, g1, w_in, mu, w_up, w0, a_up, a0, k_k, k_a, r_k, ln_g, ln_b, f_b, q_g, k_g,
                 wp_r, wp_s, wp_f, w_out, g2, wg, bg, we, be, m_gate, m_up, m_down, out):
    n2_dram = nc.dram_tensor("n2_rows", [SEQ, D], F32, kind="Internal").ap()
    y_dram = nc.dram_tensor("expert_rows", [(NE + NOV) * P, D], F32, kind="Internal").ap()

    with ExitStack() as ctx:
        def sb(name, shape, dt=F32):
            return ctx.enter_context(nc.sbuf_tensor(name, shape, dt))

        sems = {}

        def sem(name):
            if name not in sems:
                sems[name] = ctx.enter_context(nc.semaphore(name))
            return sems[name]

        ctx.enter_context(nc.allow_non_contiguous_dma("small parameter vectors"))
        ps = ctx.enter_context(nc.psum_tensor("ps", [P, 8, 512], F32))
        psf = ps[:].rearrange("p b n -> p (b n)")

        ident = sb("ident", [P, P])
        ones = sb("ones", [P, P])
        head_ones = sb("head_ones", [P, P])
        tri_le = sb("tri_le", [P, P])
        tri_lt = sb("tri_lt", [P, P])
        tri_sb = sb("tri_sb", [P, P])
        neg_sb = sb("neg_sb", [P, P])
        neg_fox = sb("neg_fox", [P, P])
        neg_ones = sb("neg_ones", [P, P])
        ident2 = sb("ident2", [P, CH])
        strict_st = sb("strict_st", [P, CH])
        strict_ts = sb("strict_ts", [P, CH])
        incl_st = sb("incl_st", [P, CH])
        lev_ts = sb("lev_ts", [P, 6, CH], U32)
        lev_st = sb("lev_st", [P, 6, CH], U32)
        reset = sb("reset", [P, L])
        chan = sb("chan", [P, 64])
        g1c, muc, w0c, a0c = chan[:, 0:8], chan[:, 8:18], chan[:, 18:21], chan[:, 21:24]
        kkc, kac, rkc = chan[:, 24:27], chan[:, 27:30], chan[:, 30:33]
        lgc, lbc = chan[:, 33:36], chan[:, 36:39]
        qgc, kgc, qg8 = chan[:, 39:40], chan[:, 40:41], chan[:, 41:42]
        up_w = sb("up_w", [P, RW])
        fb = sb("fb", [P, FH])
        rbias = sb("rbias", [P, NG + NE])
        rw = sb("rw", [P, DC, NG + NE])
        iota_f = sb("iota_f", [P, P])
        iota_row = sb("iota_row", [P, NE])
        tokid = sb("tokid", [P, NT])
        stat = sb("stat", [P, 16])
        h = sb("h", [P, NT, D])
        yT = [sb(f"yT{i}", [P, 3, SEQ]) for i in range(3)]
        ARENA = 39700
        arena = sb("arena", [P, ARENA])
        at = [0]

        def carve(shape, dt=F32, start=None):
            if start is not None:
                at[0] = start
            n = 1
            for s in shape:
                n *= s
            v = arena[:, at[0]:at[0] + n]
            at[0] += n
            assert at[0] <= ARENA, at[0]
            if len(shape) == 2:
                v = v.rearrange("p (a b) -> p a b", a=shape[0])
            if len(shape) == 3:
                v = v.rearrange("p (a b c) -> p a b c", a=shape[0], b=shape[1])
            return v

        U = carve([SC, L + 1])
        QK = carve([10, L])
        V = carve([5, 2 * SW])
        flog = carve([5, FH])
        nT = carve([DC, L])
        base = at[0]
        ring = carve([RING, DC * RING_W])
        xs = ring[:, :, 0:D]
        metax = carve([D])
        tmp_shift = carve([2, L])
        At = carve([RC, LP], start=base)
        Rt, Bt, Kt = carve([RC, LP]), carve([RC, LP]), carve([RC, LP])
        Pc = carve([RC, NCH * (CH + 1)])
        ta = carve([RC, L])
        tb = carve([RC, L])
        tc_ = carve([RC, L])
        un = [carve([NCH, CH]) for _ in range(12)]
        AtT, BtT, KtT, VT, NTm, Nm, AKT, RBT, RKT, Tm, TTm, Hm = un
        W1T = carve([NCH, CH])
        W2 = carve([NCH, CH])
        Ssb = carve([CH])
        Usb = carve([CH])
        FL = carve([FH, L], start=base)
        FR = carve([FH, L])
        fcum = carve([L])
        s_a = carve([2, SEQ])
        s_b = carve([5, SEQ])
        s_c = carve([5, SEQ])
        p_f = carve([2, L])
        pT = carve([2, 5, P])
        merged = carve([DC, SEQ], start=0)
        gsig = carve([2, SEQ])
        macc = carve([2, SEQ])
        wgr = carve([2, 3 * DC, P], start=base)
        wpr = carve([2, 9, P])
        wout = carve([DC, D])
        w1 = carve([2, DC, 2 * DE], start=0)
        w2 = carve([2, 2, D])
        xg = carve([2, D])
        xgT = carve([2, DC, P])
        hg = carve([2, 2 * DE])
        hT = carve([2, 2, P])
        yo = carve([2, D])
        Pm = carve([NT, P])
        n2 = carve([NT, D])
        n2T = carve([DC, SEQ])
        g2b = carve([D])
        rt = carve([16, NT * NE])
        ysel = carve([2, D])
        idx = sb("idx", [P, 4], U32)
        rows = sb("rows", [P, 2 * NT], U32)
        ovi = sb("ovi", [P, 2 * NOV + 2], I32)
        ovf = sb("ovf", [P, 2 * NOV + 2])

        wv = w_in.rearrange("(c p) n -> p c n", p=P)
        pieces = [("s", [(i * PIECE, PIECE)]) for i in range(SC // 2)]
        pieces += [("q", [(c, PIECE)]) for c in (C_SBQ, C_SBK, C_FQ, C_FK)]
        pieces += [("q", [(C_SBQ + 256, 64), (C_FQ + 256, 64), (C_SBK + 256, 64), (C_FK + 256, 64)])]
        pieces += [("v", [(C_SBV, SW)]), ("v", [(C_FV, FW + FH)])]
        landed = []
        for i, (_, cols) in enumerate(pieces):
            before = landed[i - RING] if i >= RING else 0
            landed.append(before + 16 * len(cols))

        def slot(i):
            return ring[:, i % RING, :].rearrange("p (c n) -> p c n", c=DC)

        def qchunk(kind, i, part):
            if i < 4:
                return {"sb": 0, "fox": 4}[kind] + 2 * part + i // 2, 64 * (i % 2)
            return 8 + part, {"sb": 0, "fox": 64}[kind]

        N_EVAC = SC + 10 + 10
        VUN = [(v, i) for v in range(2) for i in range(5)]

        block = ctx.enter_context(nc.Block())

        def follow(eng, chain):
            count = {}

            def done(ins, s=chain):
                count[s] = count.get(s, 0) + 1
                ins.then_inc(sem(s), 1)
                eng.wait_ge(sem(s), count[s])
            return done

        @block.sync
        def _(sp):
            for t in range(NT):
                sp.dma_start(h[:, t, :], x[t * P:(t + 1) * P, :]).then_inc(sem("x_in"), 16)
            sp.dma_start(metax[0:META, :], meta).then_inc(sem("x_in"), 16)
            par = sem("params_in")
            for dst, src in ((g1c, g1.rearrange("(c p) -> p c", p=P)), (muc, mu.rearrange("(c p) -> p c", p=P)),
                             (w0c, w0.rearrange("(c p) -> p c", p=P)), (a0c, a0.rearrange("(c p) -> p c", p=P)),
                             (kkc, k_k.rearrange("(c h) d -> (h d) c", h=2)),
                             (kac, k_a.rearrange("(c h) d -> (h d) c", h=2)),
                             (rkc, r_k.rearrange("(c h) d -> (h d) c", h=2)),
                             (lgc, ln_g.rearrange("(c p) -> p c", p=P)), (lbc, ln_b.rearrange("(c p) -> p c", p=P)),
                             (qgc[0:64], q_g.rearrange("(p a) -> p a", a=1)), (qgc[64:128], q_g.rearrange("(p a) -> p a", a=1)),
                             (kgc[0:64], k_g.rearrange("(p a) -> p a", a=1)), (kgc[64:128], k_g.rearrange("(p a) -> p a", a=1)),
                             (up_w[0:64, :], w_up), (up_w[64:128, :], a_up),
                             (fb[:], f_b.rearrange("(a n) -> a n", a=1).broadcast_to([P, FH])),
                             (rbias[:, 0:NG], bg.rearrange("(a n) -> a n", a=1).broadcast_to([P, NG])),
                             (rbias[:, NG:], be.rearrange("(a n) -> a n", a=1).broadcast_to([P, NE])),
                             (rw[:, :, 0:NG], wg.rearrange("(c p) n -> p c n", p=P)),
                             (rw[:, :, NG:], we.rearrange("(c p) n -> p c n", p=P))):
                sp.dma_start(dst, src).then_inc(par, 16)
            sp.wait_ge(sem("nT_ready"), DC)
            sp.wait_ge(sem("nT_meta"), 1)
            for i, (_, cols) in enumerate(pieces):
                if i >= RING:
                    sp.wait_ge(sem("piece_used"), i - RING + 1)
                col = 0
                for c0, n in cols:
                    sp.dma_start(slot(i)[:, :, col:col + n], wv[:, :, c0:c0 + n]).then_inc(sem(f"ring{i % RING}"), 16)
                    col += n
            for t in range(NOV):
                sp.dma_start(y_dram[(NE + t) * P:(NE + t + 1) * P, :], h[:, 0, :]).then_inc(sem("y_defined"), 16)
            sp.wait_ge(sem("fcum_ready"), 2)
            sp.wait_ge(sem("frow_ones"), 1)
            for hh in range(FH):
                sp.dma_start(FL[0:1, hh, :], fcum[hh:hh + 1, :]).then_inc(sem("frows"), 16)
                sp.dma_start(FR[1:2, hh, :], fcum[64 + hh:65 + hh, :]).then_inc(sem("frows"), 16)
            sp.wait_ge(sem("y_defined"), 16 * NOV)
            sp.wait_ge(sem("dve_phase"), 4)
            sp.wait_ge(sem("act_phase"), 4)
            sp.wait_ge(sem("pe_phase"), 4)
            sp.dma_start(wout[:], w_out.rearrange("(c p) n -> p c n", p=P)).then_inc(sem("wout_in"), 16)
            for dc in range(DC):
                if dc >= 2:
                    sp.wait_ge(sem("proj_used"), dc - 1)
                s = sem(f"proj_w{dc % 2}")
                for b in range(3):
                    c0 = C_G + b * D + dc * P
                    sp.dma_start(wgr[:, dc % 2, b * DC:(b + 1) * DC, :], wv[:, :, c0:c0 + P]).then_inc(s, 16)
                cs = slice(dc * P, dc * P + P)
                sp.dma_start(wpr[:, dc % 2, 0:3, :], wp_r[:, cs].rearrange("(c p) n -> p c n", p=P)).then_inc(s, 16)
                for b, w in ((1, wp_s), (2, wp_f)):
                    sp.dma_start(wpr[:, dc % 2, 3 * b:3 * b + 2, :], w[0:256, cs].rearrange("(c p) n -> p c n", p=P)).then_inc(s, 16)
                    lo = 64 * (b - 1)
                    sp.dma_start(wpr[lo:lo + 64, dc % 2, 3 * b + 2, :], w[256:320, cs]).then_inc(s, 16)
            sp.wait_ge(sem("pe_phase"), 5)
            sp.wait_ge(sem("dve_phase"), 5)
            sp.wait_ge(sem("act_phase"), 5)
            sp.dma_start(g2b[:], g2.rearrange("(a n) -> a n", a=1).broadcast_to([P, D])).then_inc(sem("g2_in"), 16)
            for t in range(NE):
                if t == 2:
                    for i in range(NT):
                        sp.wait_ge(sem("n2_ready"), i + 1)
                        sp.dma_start(n2_dram[i * P:(i + 1) * P, :], n2[:, i, :]).then_inc(sem("n2_out"), 16)
                if t >= 2:
                    sp.wait_ge(sem("gu_psum"), t - 1)
                s = t % 2
                sp.dma_start(w1[:, s, :, 0:DE], m_gate[t, :, :].rearrange("(c p) n -> p c n", p=P)).then_inc(sem(f"moe_w{s}"), 16)
                sp.dma_start(w1[:, s, :, DE:], m_up[t, :, :].rearrange("(c p) n -> p c n", p=P)).then_inc(sem(f"moe_w{s}"), 16)
                if t >= 2:
                    sp.wait_ge(sem("down_psum"), t - 1)
                sp.dma_start(w2[:, s, :, :], m_down[t, :, :].rearrange("(c p) n -> p c n", p=P)).then_inc(sem(f"moe_d{s}"), 16)
                if t >= 2:
                    sp.wait_ge(sem("y_low"), t - 1)
                    sp.wait_ge(sem("y_high"), t - 1)
                    sp.dma_start(y_dram[(t - 2) * P:(t - 1) * P, :], yo[:, t % 2, :]).then_inc(sem(f"y_out{t % 2}"), 16)
            for t in range(NE - 2, NE):
                sp.wait_ge(sem("y_low"), t + 1)
                sp.wait_ge(sem("y_high"), t + 1)
                sp.dma_start(y_dram[t * P:(t + 1) * P, :], yo[:, t % 2, :]).then_inc(sem(f"y_out{t % 2}"), 16)
            sp.wait_ge(sem("ov_ready"), 1)
            sp.wait_ge(sem("y_defined"), 16 * NOV)
            n_ov = sp.value_load(ovi[0:1, 0:1], min_val=0, max_val=NOV)
            with sp.Fori(0, NOV) as k:
                with sp.If(k < n_ov):
                    e = sp.value_load(ovi[0:1, bass.ds(k + 1, 1)], min_val=0, max_val=NE - 1)
                    sp.wait_ge(sem("down_psum"), k + NE)
                    for dst, src, ready in ((w1[:, 0, :, 0:DE], m_gate, sem("moe_w0")), (w1[:, 0, :, DE:], m_up, sem("moe_w0")),
                                            (w2[:, 0, :, :], m_down, sem("moe_d0"))):
                        sp.dma_start(dst, src[bass.ds(e, 1), :, :].rearrange("e (c p) n -> p (e c) n", p=P)).then_inc(ready, 16)
                    sp.wait_ge(sem("y_low"), k + NE + 1)
                    sp.wait_ge(sem("y_high"), k + NE + 1)
                    sp.dma_start(y_dram.rearrange("(t p) n -> t p n", p=P)[bass.ds(k + NE, 1), :, :].rearrange("t p n -> p (t n)"),
                                 yo[:, 0, :]).then_inc(sem("y_out0"), 16)
            sp.wait_ge(sem("y_out0"), n_ov * 16 + NE * 8)
            sp.wait_ge(sem("y_out1"), NE * 8)
            sp.sem_inc(sem("y_stored"), 1)
            for t in range(NT):
                sp.wait_ge(sem("out_ready"), t + 1)
                sp.dma_start(out[t * P:(t + 1) * P, :], h[:, t, :]).then_inc(sem("out_out"), 16)
            sp.wait_ge(sem("out_out"), 16 * NT)
            sp.wait_ge(sem("n2_out"), 16 * NT)

        @block.gpsimd
        def _(pool):
            done = follow(pool, "pool_chain")
            g = nc.gpsimd

            def masked(ap, fill_in, op, pattern, base_, mult, fill=0.0):
                done(g.memset(ap, fill_in))
                done(g.affine_select(out=ap, in_=ap, pattern=pattern, compare_op=op, fill=fill, base=base_,
                                     channel_multiplier=mult))

            done(g.memset(ident[:], 1.0))
            done(g.affine_select(out=ident[:], in_=ident[:], pattern=[[1, P]], compare_op=ALU.is_equal, fill=0.0, base=0,
                                 channel_multiplier=-1), "ident_ready")
            done(g.memset(ones[:], 1.0))
            done(g.memset(neg_ones[:], -1.0))
            masked(tri_le[:], 1.0, ALU.is_ge, [[1, P]], 0, -1)
            masked(tri_lt[:], 1.0, ALU.is_gt, [[1, P]], 0, -1)
            masked(tri_sb[:], -1.0, ALU.is_ge, [[-1, P]], 0, 1)
            masked(neg_sb[:], 0.0, ALU.is_gt, [[1, P]], 0, -1, NEG)
            masked(neg_fox[:], 0.0, ALU.is_ge, [[-1, P]], 0, 1, NEG)
            done(g.memset(head_ones[:], 0.0))
            for i in range(2):
                done(g.memset(head_ones[64 * i:64 * i + 64, 64 * i:64 * i + 64], 1.0))
            for i in range(2):
                q = slice(64 * i, 64 * i + 64)
                masked(ident2[q, :], 1.0, ALU.is_equal, [[1, CH]], 0, -1)
                masked(strict_st[q, :], 1.0, ALU.is_gt, [[1, CH]], 0, -1)
                masked(strict_ts[q, :], 1.0, ALU.is_gt, [[-1, CH]], 0, 1)
                masked(incl_st[q, :], 1.0, ALU.is_ge, [[1, CH]], 0, -1)
            for lv in range(6):
                m = 1 << lv
                nb = CH // (2 * m)
                for i in range(2):
                    q = slice(64 * i, 64 * i + 64)
                    a = Hm[q, lv, :].rearrange("p (b w) -> p b w", b=nb)
                    done(g.memset(a, 1.0))
                    done(g.affine_select(out=a, in_=a, pattern=[[-2 * m, nb], [0, 2 * m]], compare_op=ALU.is_ge, fill=0.0, base=-m, channel_multiplier=1))
                    done(g.affine_select(out=a, in_=a, pattern=[[2 * m, nb], [0, 2 * m]], compare_op=ALU.is_gt, fill=0.0, base=2 * m, channel_multiplier=-1))
                    done(g.affine_select(out=a, in_=a, pattern=[[0, nb], [-1, 2 * m]], compare_op=ALU.is_gt, fill=0.0, base=m, channel_multiplier=0))
                    done(g.tensor_copy(lev_ts[q, lv, :], Hm[q, lv, :]))
                    done(g.memset(a, 1.0))
                    done(g.affine_select(out=a, in_=a, pattern=[[2 * m, nb], [0, 2 * m]], compare_op=ALU.is_gt, fill=0.0, base=m, channel_multiplier=-1))
                    done(g.affine_select(out=a, in_=a, pattern=[[-2 * m, nb], [0, 2 * m]], compare_op=ALU.is_ge, fill=0.0, base=0, channel_multiplier=1))
                    done(g.affine_select(out=a, in_=a, pattern=[[0, nb], [1, 2 * m]], compare_op=ALU.is_ge, fill=0.0, base=-m, channel_multiplier=0))
                    done(g.tensor_copy(lev_st[q, lv, :], Hm[q, lv, :]))
            done(g.memset(reset[:], 1.0))
            done(g.memset(reset[:, 0:L:CH], 0.0))
            done(g.iota(iota_f[:], [[1, P]], base=0, channel_multiplier=0, allow_small_or_imprecise_dtypes=True))
            done(g.iota(iota_row[:], [[1, NE]], base=0, channel_multiplier=0, allow_small_or_imprecise_dtypes=True))
            done(g.iota(tokid[:], [[P, NT]], base=0, channel_multiplier=1, allow_small_or_imprecise_dtypes=True), "consts_ready")
            pool.wait_ge(sem("n2_out"), 16 * NT)
            for t in range(NE):
                pool.wait_ge(sem("idx_ready"), t + 1)
                if t >= 2:
                    pool.wait_ge(sem("xgT_psum"), 2 * t - 2)
                g.indirect_dma_start(out=xg[:, t % 2, :], out_offset=None, in_=n2_dram[:, :],
                                     in_offset=bass.IndirectOffsetOnAxis(ap=idx[:, t % 2:t % 2 + 1], axis=0)).then_inc(sem(f"xg_in{t % 2}"), 16)
            pool.wait_ge(sem("ov_ready"), 1)
            n_ov = pool.value_load(ovi[0:1, 0:1], min_val=0, max_val=NOV)
            with pool.Fori(0, NOV) as k:
                with pool.If(k < n_ov):
                    pool.wait_ge(sem("idx_ready"), k + NE + 1)
                    pool.sem_inc(sem("pool_go"), 1)
                    g.indirect_dma_start(out=xg[:, 0, :], out_offset=None, in_=n2_dram[:, :],
                                         in_offset=bass.IndirectOffsetOnAxis(ap=idx[:, 0:1], axis=0)).then_inc(sem("xg_in0"), 16)
            pool.wait_ge(sem("y_stored"), 1)
            for t in range(NT):
                for j in range(2):
                    if t >= 1:
                        pool.wait_ge(sem("ysel_used"), 2 * (t - 1) + j + 1)
                    g.indirect_dma_start(out=ysel[:, j, :], out_offset=None, in_=y_dram[:, :],
                                         in_offset=bass.IndirectOffsetOnAxis(ap=rows[:, 2 * t + j:2 * t + j + 1], axis=0)).then_inc(sem(f"ysel_in{j}"), 16)

        @block.scalar
        def _(act):
            a = nc.scalar
            done = follow(act, "act_chain")

            def inverse_root(z, s, scale=1.0):
                a.preload_act_table_set("natural_log")
                done(a.activation(z, z, ACT.Ln, scale=scale))
                done(a.activation(z, z, ACT.Exp, scale=-0.5), s)
            act.wait_ge(sem("x_in"), 16 * (NT + 1))
            for t in range(NT):
                done(a.activation(xs[:, t, :], h[:, t, :], ACT.Square, accum_out=stat[:, t:t + 1]), "ss_ready")
            done(a.activation(tmp_shift[0:META, :, :].rearrange("p a b -> p (a b)")[:, 0:D], metax[0:META, :], ACT.Square,
                              accum_out=stat[0:META, 4:5]), "ss_ready")
            act.wait_ge(sem("ms_ready"), 2)
            inverse_root(stat[:, 0:4], "rstd_ready")
            inverse_root(stat[0:META, 4:5], "rstd_ready")
            act.wait_ge(sem("params_in"), 320)
            done(a.mul(qg8, qgc, 0.125), "qg8_ready")
            for c in range(DC):
                act.wait_ge(sem("xT_psum"), c + 1)
                done(a.activation(nT[:, c, META:L], ps[:, c % 4, :], ACT.Copy, scale=g1c[:, c:c + 1]), "nT_ready")
            n = 0
            for j in range(SC):
                act.wait_ge(sem("chunk_psum"), n + 1)
                done(a.activation(U[:, j, 1:L + 1].rearrange("p (a b) -> p a b", a=2), ps[:, 2 * (n % 2):2 * (n % 2) + 2, 0:HALF], ACT.Copy), "chunk_out")
                n += 1
            for j in range(10):
                act.wait_ge(sem("chunk_psum"), n + 1)
                pin = ps[:, 2 * (n % 2):2 * (n % 2) + 2, 0:HALF]
                dst = QK[:, j, :].rearrange("p (a b) -> p a b", a=2)
                if j < 8 or j == 9:
                    done(a.activation(dst, pin, ACT.Copy, scale=0.125 if j < 2 else 1.0), "chunk_out")
                else:
                    done(a.activation(dst[0:64], pin[0:64], ACT.Copy, scale=0.125))
                    done(a.activation(dst[64:128], pin[64:128], ACT.Copy), "chunk_out")
                n += 1
            for v, i in VUN:
                r = KT[i][1]
                act.wait_ge(sem("chunk_psum"), n + 1)
                if v == 0:
                    done(a.activation(V[0:r, i, 0:SW], ps[0:r, n % 4, 0:SW], ACT.Copy), "chunk_out")
                else:
                    done(a.activation(V[0:r, i, SW:], ps[0:r, n % 4, 0:SW], ACT.Copy))
                    done(a.activation(flog[0:r, i, :], ps[0:r, n % 4, SW:SW + FH], ACT.Copy), "chunk_out")
                n += 1
            for m, j in enumerate((4, 5, 6, 7, 8, 9)):
                if m >= 1:
                    act.wait_ge(sem("norm_psum"), m)
                done(a.activation(tmp_shift[:, 0, :], QK[:, j, :], ACT.Square), "fsq_ready")
                act.wait_ge(sem("fms_ready"), m + 1)
                inverse_root(tmp_shift[slice(0, P) if j < 8 else slice(64, P), 1, :], "frs_ready")
            act.wait_ge(sem("norm_psum"), 6)
            a.sem_inc(sem("act_phase"), 1) if False else done(a.activation(stat[:, 8:9], stat[:, 0:1], ACT.Copy), "act_phase")

            act.wait_ge(sem("dve_phase"), 1)
            act.wait_ge(sem("pe_phase"), 1)
            done(a.activation(U[0:64, 9, 1:], U[0:64, 9, 1:], ACT.Tanh), "wd_ready")
            for c in range(RC):
                act.wait_ge(sem("wa_psum"), 2 * c + 1)
                pin = psf[:, 0:1024].rearrange("p (a b) -> p a b", a=2)[:, :, 0:HALF]
                done(a.activation(ta[:, c, :].rearrange("p (a b) -> p a b", a=2), pin, ACT.Sigmoid, bias=w0c[:, c:c + 1]), "wa_used")
                act.wait_ge(sem("wa_psum"), 2 * c + 2)
                pin = psf[:, 1024:2048].rearrange("p (a b) -> p a b", a=2)[:, :, 0:HALF]
                done(a.activation(tb[:, c, :].rearrange("p (a b) -> p a b", a=2), pin, ACT.Sigmoid, bias=a0c[:, c:c + 1]), "wa_used")
            for c in range(RC):
                act.wait_ge(sem("kk_used"), c + 1)
                inverse_root(Kt[:, c, 0:L], "kk_rs", float(2 ** 30))
            act.wait_ge(sem("cum_ready"), RC)
            for c in range(RC):
                pv = Pc[:, c, :].rearrange("p (n t) -> p n t", t=CH + 1)
                done(a.activation(pv[:, 0:NCH - 1, 1:], tc_[:, c, 0:(NCH - 1) * CH].rearrange("p (n t) -> p n t", t=CH), ACT.Exp, scale=-DECAY))
                done(a.activation(pv[:, NCH - 1, 1:1 + L % CH], tc_[:, c, (NCH - 1) * CH:L], ACT.Exp, scale=-DECAY))
                done(a.activation(tc_[:, c, :], tc_[:, c, :], ACT.Exp, scale=DECAY), "decay_ready")
            for p in range(RC):
                for q, dst in enumerate((AtT, BtT, KtT, VT)):
                    act.wait_ge(sem("tr_psum"), 4 * p + q + 1)
                    done(a.activation(dst.rearrange("p n t -> p (n t)"), psf[:, 1024 * (q % 2):1024 * (q % 2) + LP], ACT.Copy), "tr_used")
                for lv in range(1, 6):
                    act.wait_ge(sem("H_psum"), 5 * p + lv)
                    done(a.activation(Hm.rearrange("p n t -> p (n t)"), psf[:, 2048:2048 + LP], ACT.Copy), "H_ready")
                act.wait_ge(sem("w1_psum"), p + 1)
                done(a.activation(W1T.rearrange("p n t -> p (n t)"), psf[:, 0:LP], ACT.Copy), "w1_ready")
                act.wait_ge(sem("akv_psum"), p + 1)
                done(a.activation(Hm.rearrange("p n t -> p (n t)"), psf[:, 1024:1024 + LP], ACT.Copy), "akv_ready")
                act.wait_ge(sem("w2_psum"), p + 1)
                done(a.activation(W2.rearrange("p n t -> p (n t)"), psf[:, 2048:2048 + LP], ACT.Copy), "w2_ready")
                for c in range(NCH):
                    act.wait_ge(sem("y_psum"), NCH * p + c + 1)
                    w = min(CH, L - c * CH)
                    done(a.activation(ta[:, p, c * CH:c * CH + w], ps[:, 5 + 2 * (c % 2), 0:w], ACT.Copy), "y_out_rwkv")
            done(a.activation(tb[:].rearrange("p a b -> p (a b)"), ta[:].rearrange("p a b -> p (a b)"), ACT.Square), "act_phase")
            for c in range(RC):
                act.wait_ge(sem("var_ready"), c + 1)
                inverse_root(Kt[:, c, 0:L], "ln_rs")

            act.wait_ge(sem("dve_phase"), 2)
            act.wait_ge(sem("pe_phase"), 2)
            act.wait_ge(sem("f_pre"), 1)
            fl = flog.rearrange("p a b -> p (a b)")
            done(a.activation(fl[:, 0:20], fl[:, 0:20], ACT.Exp, scale=-1.0))
            done(a.activation(fl[0:16, 20:25], fl[0:16, 20:25], ACT.Exp, scale=-1.0))
            done(a.activation(fl[:, 0:20], fl[:, 0:20], ACT.Ln, bias=1.0))
            done(a.activation(fl[0:16, 20:25], fl[0:16, 20:25], ACT.Ln, bias=1.0), "f_ready")
            act.wait_ge(sem("fcum_psum"), 1)
            pin = psf[:, 0:1024].rearrange("p (a b) -> p a b", a=2)[0:FH, :, 0:HALF]
            done(a.activation(fcum[0:FH, :].rearrange("p (a b) -> p a b", a=2), pin, ACT.Copy, scale=-1.0), "fcum_ready")
            done(a.activation(fcum[64:64 + FH, :].rearrange("p (a b) -> p a b", a=2), pin, ACT.Copy), "fcum_ready")
            a.preload_act_table_set("natural_log_exp_and_others")
            u = 0
            for hh in range(SH):
                for i, (k0, r) in enumerate(KT):
                    n = min(SEQ, L - k0)
                    act.wait_ge(sem("z_psum"), u + 1)
                    if hh >= 1:
                        act.wait_ge(sem("sb_used"), hh)
                    if u >= 2:
                        act.wait_ge(sem("sp_ready"), u - 1)
                    e = s_a[0:r, u % 2, 0:n]
                    z = ps[0:r, i, 0:n]
                    done(a.activation(e, z, ACT.Abs))
                    done(a.activation(e, e, ACT.Exp, scale=-1.0))
                    done(a.activation(e, e, ACT.Ln, bias=1.0), "l_ready")
                    u += 1
                for i, (k0, r) in enumerate(KT):
                    n = min(SEQ, L - k0)
                    act.wait_ge(sem("w_psum"), 5 * hh + i + 1)
                    done(a.activation(s_c[0:r, i, 0:n], ps[0:r, i, 0:n], ACT.Exp), "A_ready")
            done(a.activation(stat[:, 8:9], stat[:, 0:1], ACT.Copy), "act_phase")

            act.wait_ge(sem("dve_phase"), 3)
            u = 0
            for hh in range(FH):
                for i in range(NT):
                    kn = META + P * (i + 1)
                    act.wait_ge(sem("m_ready"), u + 1)
                    if u >= 2:
                        act.wait_ge(sem("pT_psum"), u - 1)
                    done(a.activation(p_f[:, u % 2, 0:kn], psf[:, 1024 * (u % 2):1024 * (u % 2) + kn], ACT.Exp,
                                      bias=stat[:, 9 + u % 2:10 + u % 2], accum_out=stat[:, 11 + u % 2:12 + u % 2]), "p_ready")
                    u += 1
            act.wait_ge(sem("pT_psum"), u)
            done(a.activation(stat[:, 8:9], stat[:, 0:1], ACT.Copy), "act_phase")

            act.wait_ge(sem("dve_phase"), 4)
            n = 0
            for dc in range(DC):
                for b in range(3):
                    act.wait_ge(sem("gate_psum"), n + 1)
                    if n >= 2:
                        act.wait_ge(sem("gsig_used"), n - 1)
                    done(a.activation(gsig[:, n % 2, :], ps[:, n % 2, :], ACT.Sigmoid), "gsig_ready")
                    n += 1
            done(a.activation(stat[:, 8:9], stat[:, 0:1], ACT.Copy), "act_phase")

            act.wait_ge(sem("dve_phase"), 5)
            for t in range(NT):
                act.wait_ge(sem("h_ready"), t + 1)
                done(a.activation(n2[:, t, :], h[:, t, :], ACT.Square, accum_out=stat[:, t:t + 1]), "ss2_ready")
            act.wait_ge(sem("ms2_ready"), 1)
            inverse_root(stat[:, 0:4], "rstd2_ready")
            for c in range(DC):
                act.wait_ge(sem("n2T_psum"), c + 1)
                done(a.activation(n2T[:, c, :], ps[:, c % 2, :], ACT.Copy), "n2T_ready")
            act.wait_ge(sem("lg_ready"), 1)
            done(a.activation(rt[:, 1, 0:NT * NG], rt[:, 1, 0:NT * NG], ACT.Exp))
            done(a.activation(rt[:, 2, 0:NT], rt[:, 2, 0:NT], ACT.Exp), "pe_exp")

            def rows_T(t, s, slot_free):
                for k in range(2):
                    act.wait_ge(sem("xgT_psum"), t * 2 + (k + 1))
                    if slot_free:
                        act.wait_ge(sem("gu_psum"), t - 1)
                    a.activation(xgT[:, s, 4 * k:4 * k + 4, :].rearrange("p c n -> p (c n)"), ps[:, k, :], ACT.Copy).then_inc(sem("xgT_ready"), 1)

            def silu(t, s, bank, slot_free):
                act.wait_ge(sem("gu_psum"), t + 1)
                if slot_free:
                    act.wait_ge(sem("hT_psum"), t - 1)
                a.activation(hg[:, s, 0:DE], ps[:, bank, 0:DE], ACT.Silu).then_inc(sem("silu_ready"), 1)

            def hidden_T(t, s, slot_free):
                act.wait_ge(sem("hT_psum"), t + 1)
                if slot_free:
                    act.wait_ge(sem("down_psum"), t - 1)
                a.activation(hT[:, s, :, :].rearrange("p c n -> p (c n)"), ps[:, 3, 0:2 * P], ACT.Copy).then_inc(sem("hT_ready"), 1)

            def y_low(t, s, stores):
                act.wait_ge(sem("down_psum"), t + 1)
                if stores is not None:
                    act.wait_ge(sem(f"y_out{s}"), stores)
                a.activation(yo[:, s, 0:512], ps[:, 4, :], ACT.Copy).then_inc(sem("y_low"), 1)
            rows_T(0, 0, False)
            for t in range(NE + 1):
                if t < NE:
                    silu(t, t % 2, 2 + 4 * (t % 2), t >= 2)
                if t >= 1:
                    hidden_T(t - 1, (t - 1) % 2, t >= 3)
                if t + 1 < NE:
                    rows_T(t + 1, (t + 1) % 2, t >= 1)
                if t >= 1:
                    y_low(t - 1, (t - 1) % 2, 16 * ((t - 1) // 2) if t >= 3 else None)
            act.wait_ge(sem("ov_ready"), 1)
            n_ov = act.value_load(ovi[0:1, 0:1], min_val=0, max_val=NOV)
            with act.Fori(0, NOV) as k:
                with act.If(k < n_ov):
                    t = k + NE
                    act.wait_ge(sem("y_out0"), k * 16 + NE * 8)
                    rows_T(t, 0, False)
                    silu(t, 0, 2, False)
                    hidden_T(t, 0, False)
                    y_low(t, 0, None)

        @block.vector
        def _(dve):
            v = nc.vector
            done = follow(dve, "dve_chain")
            ts, tt, stt = v.tensor_scalar, v.tensor_tensor, v.scalar_tensor_tensor
            dve.wait_ge(sem("ss_ready"), NT + 1)
            done(ts(stat[:, 0:4], stat[:, 0:4], 1.0 / D, EPS, ALU.mult, ALU.add), "ms_ready")
            done(ts(stat[0:META, 4:5], stat[0:META, 4:5], 1.0 / D, EPS, ALU.mult, ALU.add), "ms_ready")
            dve.wait_ge(sem("rstd_ready"), 2)
            for t in range(NT):
                done(ts(xs[:, t, :], h[:, t, :], stat[:, t:t + 1], None, ALU.mult), "xs_ready")
            done(ts(metax[0:META, :], metax[0:META, :], stat[0:META, 4:5], None, ALU.mult), "xs_ready")
            dve.wait_ge(sem("params_in"), 320)
            dve.wait_ge(sem("xT_psum"), DC + 1)
            done(tt(nT[:, :, 0:META], ps[:, 4, 0:DC * META].rearrange("p (c n) -> p c n", c=DC),
                    g1c.rearrange("p (c a) -> p c a", a=1).broadcast_to([P, DC, META]), ALU.mult), "nT_meta")
            for j in range(SC):
                done(v.memset(U[:, j, 0:1], 0.0))
            for j in range(SC):
                dve.wait_ge(sem("chunk_out"), j + 1)
                d_ = tmp_shift[:, 1, :]
                done(tt(d_, U[:, j, 0:L], U[:, j, 1:L + 1], ALU.subtract))
                done(stt(U[:, j, 1:L + 1], d_, muc[:, j:j + 1], U[:, j, 1:L + 1], ALU.mult, ALU.add))
            dve.wait_ge(sem("qg8_ready"), 1)
            for m, j in enumerate((4, 5, 6, 7, 8, 9)):
                dve.wait_ge(sem("norm_psum"), m + 1)
                d_ = tmp_shift[:, 1, :].rearrange("p (a b) -> p a b", a=2)
                gain = (qg8, qg8, kgc, kgc, qg8, kgc)[m]
                q = slice(0, P) if j < 8 else slice(64, P)
                o = 4 * (m % 2)
                done(ts(d_[q], ps[q, o:o + 2, 0:HALF], 1.0 / HD, EPS, ALU.mult, ALU.add), "fms_ready")
                dve.wait_ge(sem("frs_ready"), m + 1)
                done(stt(QK[q, j, :], QK[q, j, :], gain[q], tmp_shift[q, 1, :], ALU.mult, ALU.mult), "norm_used")
            dve.wait_ge(sem("chunk_out"), N_EVAC)
            done(tt(flog[:, 0:4, :], flog[:, 0:4, :], fb[:].rearrange("p (a n) -> p a n", a=1).broadcast_to([P, 4, FH]), ALU.add))
            done(tt(flog[0:16, 4, :], flog[0:16, 4, :], fb[0:16, :], ALU.add), "f_pre")
            done(v.memset(stat[:, 13:14], 0.0), "dve_phase")

            dve.wait_ge(sem("act_phase"), 1)
            dve.wait_ge(sem("pe_phase"), 1)
            r_, k_, v_ = U[:, 0:3, 1:], U[:, 3:6, 1:], U[:, 6:9, 1:]
            for t_ in (At, Rt, Bt, Kt):
                done(v.memset(t_[:, :, L:LP], 0.0))
            done(v.memset(Pc[:], 1.0))
            dve.wait_ge(sem("consts_ready"), 1)
            for c in range(RC):
                dve.wait_ge(sem("wa_used"), 2 * c + 1)
                done(v.tensor_tensor_scan(tc_[:, c, :], reset[:], ta[:, c, :], 0.0, ALU.mult, ALU.add), "cum_ready")
            for c in range(RC):
                done(ts(At[:, c, 0:L], k_[:, c, :], kkc[:, c:c + 1], None, ALU.mult))
                done(tt(Bt[:, c, 0:L], At[:, c, 0:L], At[:, c, 0:L], ALU.mult), "kk_sq")
            for c in range(RC):
                dve.wait_ge(sem("kk_psum"), c + 1)
                d_ = Kt[:, c, 0:L].rearrange("p (a b) -> p a b", a=2)
                done(ts(d_, psf[:, 2048:3072].rearrange("p (a b) -> p a b", a=2)[:, :, 0:HALF], 1e-24, None, ALU.max), "kk_used")
            AL, RL, BL, KL = (z[:, :, 0:L] for z in (At, Rt, Bt, Kt))
            dve.wait_ge(sem("kk_rs"), RC)
            done(stt(AL, AL, 32768.0, KL, ALU.mult, ALU.mult))
            dve.wait_ge(sem("wa_used"), 2 * RC)
            done(tt(BL, AL, tb[:], ALU.mult))
            for c in range(RC):
                done(ts(tb[:, c, :], tb[:, c, :], 1.0, kac[:, c:c + 1], ALU.subtract, ALU.mult))
                done(stt(KL[:, c, :], tb[:, c, :], 1.0, k_[:, c, :], ALU.add, ALU.mult))
                done(stt(tb[:, c, :], r_[:, c, :], rkc[:, c:c + 1], KL[:, c, :], ALU.mult, ALU.mult), "rk_ready")
            dve.wait_ge(sem("decay_ready"), RC)
            for c in range(RC):
                pv = Pc[:, c, :].rearrange("p (n t) -> p n t", t=CH + 1)
                for dst, src, o, sgn in ((At, At, 0, -1.0), (Rt, None, 1, 1.0)):
                    for n0, n1, w in ((0, NCH - 1, CH), (NCH - 1, NCH, L % CH)):
                        lo = n0 * CH
                        hi = lo + (n1 - n0) * w
                        so = dst[:, c, lo:hi].rearrange("p (n t) -> p n t", t=w)
                        si = so if src is not None else r_[:, c, lo:hi].rearrange("p (n t) -> p n t", t=w)
                        done(stt(so, si, sgn, pv[:, n0:n1, o:o + w], ALU.mult, ALU.mult))
            done(tt(BL, BL, tc_[:], ALU.mult))
            done(tt(KL, KL, tc_[:], ALU.mult), "tilde_ready")
            for c in range(RC):
                dve.wait_ge(sem("bonus_psum"), c + 1)
                done(tt(tb[:, c, :].rearrange("p (a b) -> p a b", a=2), psf[:, 2048:3072].rearrange("p (a b) -> p a b", a=2)[:, :, 0:HALF],
                        v_[:, c, :].rearrange("p (a b) -> p a b", a=2), ALU.mult), "bonus_used")
            done(v.tensor_copy(tc_[:], tb[:]))
            bc = lambda m_: m_.rearrange("p (a t) -> p a t", a=1).broadcast_to([P, NCH, CH])
            for p in range(RC):
                for q, (dst, msk) in enumerate(((AKT, strict_st), (RKT, incl_st), (NTm, strict_st), (RBT, incl_st), (Nm, strict_ts))):
                    dve.wait_ge(sem("g_psum"), 5 * p + q + 1)
                    done(tt(dst[:], psf[:, 1024 * (2 + q % 2):1024 * (2 + q % 2) + LP].rearrange("p (n t) -> p n t", t=CH), bc(msk[:]), ALU.mult), "g_used")
                done(v.tensor_copy(Tm[:], bc(ident2[:])))
                done(v.copy_predicated(Tm[:], bc(lev_ts[:, 0, :]), Nm[:]))
                done(v.tensor_copy(TTm[:], bc(ident2[:])))
                done(v.copy_predicated(TTm[:], bc(lev_st[:, 0, :]), NTm[:]), "T_ready")
                for lv in range(1, 6):
                    if lv < 5:
                        dve.wait_ge(sem("G_psum"), 9 * p + 2 * lv - 1)
                        done(v.copy_predicated(Tm[:], bc(lev_ts[:, lv, :]), psf[:, 3072:3072 + LP].rearrange("p (n t) -> p n t", t=CH)))
                    dve.wait_ge(sem("G_psum"), 9 * p + min(2 * lv, 9))
                    done(v.copy_predicated(TTm[:], bc(lev_st[:, lv, :]), psf[:, 0:LP].rearrange("p (n t) -> p n t", t=CH)), "T_ready")
                done(v.memset(Ssb[:], 0.0), "S_ready")
                for c in range(NCH):
                    dve.wait_ge(sem("u_psum"), NCH * p + c + 1)
                    if c == 0:
                        dve.wait_ge(sem("w2_ready"), p + 1)
                    done(tt(Usb[:], ps[:, 6, 0:CH], W2[:, c, :], ALU.add), "U_ready")
                    if c < NCH - 1:
                        dve.wait_ge(sem("s_psum"), (NCH - 1) * p + c + 1)
                        done(tt(Ssb[:], ps[:, 6, 128:128 + CH], Ssb[:], ALU.add))
                        done(ts(Ssb[:], Ssb[:], Pc[:, p, c * (CH + 1) + CH:(c + 1) * (CH + 1)], None, ALU.mult), "S_ready")
            dve.wait_ge(sem("act_phase"), 2)
            for c in range(RC):
                dve.wait_ge(sem("ln_psum"), 2 * c + 2)
                mean = Bt[:, c, 0:L].rearrange("p (a b) -> p a b", a=2)
                var = Kt[:, c, 0:L].rearrange("p (a b) -> p a b", a=2)
                done(ts(mean, psf[:, 0:1024].rearrange("p (a b) -> p a b", a=2)[:, :, 0:HALF], 1.0 / HD, None, ALU.mult))
                done(tt(At[:, c, 0:L], Bt[:, c, 0:L], Bt[:, c, 0:L], ALU.mult))
                done(stt(var, psf[:, 1024:2048].rearrange("p (a b) -> p a b", a=2)[:, :, 0:HALF], 1.0 / HD,
                         At[:, c, 0:L].rearrange("p (a b) -> p a b", a=2), ALU.mult, ALU.subtract), "ln_used")
                done(ts(Kt[:, c, 0:L], Kt[:, c, 0:L], 0.0, LN_EPS, ALU.max, ALU.add), "var_ready")
                dve.wait_ge(sem("ln_rs"), c + 1)
                done(tt(ta[:, c, :], ta[:, c, :], Bt[:, c, 0:L], ALU.subtract))
                done(tt(ta[:, c, :], ta[:, c, :], Kt[:, c, 0:L], ALU.mult))
                done(ts(ta[:, c, :], ta[:, c, :], lgc[:, c:c + 1], lbc[:, c:c + 1], ALU.mult, ALU.add))
                done(tt(yT[0][:, c, :], ta[:, c, META:], tc_[:, c, META:], ALU.add))
            done(v.memset(stat[:, 13:14], 0.0), "dve_phase")

            dve.wait_ge(sem("pe_phase"), 2)
            done(v.memset(FL[0:2, :, :], 1.0))
            done(v.memset(FR[0:2, :, :], 1.0), "frow_ones")
            u = 0
            for hh in range(SH):
                for i, (k0, r) in enumerate(KT):
                    n = min(SEQ, L - k0)
                    dve.wait_ge(sem("l_ready"), u + 1)
                    if hh >= 1:
                        dve.wait_ge(sem("w_psum"), 5 * hh)
                    done(stt(s_b[0:r, i, 0:n], ps[0:r, i, 0:n], 0.0, s_a[0:r, u % 2, 0:n], ALU.max, ALU.add))
                    q0 = META if i == 0 else 0
                    w = r - q0
                    done(tt(s_b[0:r, i, 0:w], s_b[0:r, i, 0:w], tri_lt[0:r, q0:q0 + w], ALU.mult), "sp_ready")
                    u += 1
                dve.wait_ge(sem("o_psum"), hh + 1)
                row = 64 * (hh % 2) if hh < 4 else 0
                done(v.tensor_copy(yT[1][row:row + 64, hh // 2, :], ps[row:row + 64, 6, :]), "sb_used")
            done(v.memset(stat[:, 13:14], 0.0), "dve_phase")

            dve.wait_ge(sem("act_phase"), 3)
            u = 0
            for hh in range(FH):
                for i in range(NT):
                    kn = META + P * (i + 1)
                    dve.wait_ge(sem("s_ready"), u + 1)
                    if u >= 2:
                        dve.wait_ge(sem("p_ready"), u - 1)
                    done(v.tensor_reduce(stat[:, 9 + u % 2:10 + u % 2], psf[:, 1024 * (u % 2):1024 * (u % 2) + kn], AX, ALU.max, negate=True), "m_ready")
                    dve.wait_ge(sem("p_ready"), u + 1)
                    done(v.reciprocal(stat[:, 14:15], stat[:, 11 + u % 2:12 + u % 2]))
                    done(ts(p_f[:, u % 2, 0:kn], p_f[:, u % 2, 0:kn], stat[:, 14:15], None, ALU.mult), "pn_ready")
                    dve.wait_ge(sem("pT_psum"), u + 1)
                    if u >= 2:
                        dve.wait_ge(sem("of_psum"), u - 1)
                    nk = i + 1
                    done(v.tensor_copy(pT[:, u % 2, 0:nk, :], ps[:, 4, 0:nk * P].rearrange("p (a b) -> p a b", b=P)))
                    done(v.tensor_copy(pT[0:16, u % 2, nk, :], ps[0:16, 5, 0:P]), "pTs_ready")
                    dve.wait_ge(sem("of_psum"), u + 1)
                    row = 64 * (hh % 2) if hh < 4 else 64
                    done(v.tensor_copy(yT[2][row:row + 64, hh // 2, i * P:(i + 1) * P], ps[row:row + 64, 6, 0:P]), "of_used")
                    u += 1
            done(v.memset(stat[:, 13:14], 0.0), "dve_phase")

            dve.wait_ge(sem("act_phase"), 4)
            dve.wait_ge(sem("pe_phase"), 4)
            n = 0
            for dc in range(DC):
                for b in range(3):
                    dve.wait_ge(sem("gsig_ready"), n + 1)
                    dve.wait_ge(sem("proj_psum"), n + 1)
                    dst = merged[:, dc, :] if b == 0 else macc[:, 0, :]
                    done(tt(dst, gsig[:, n % 2, :], ps[:, 2 + n % 2, :], ALU.mult), "gsig_used")
                    if b > 0:
                        done(tt(merged[:, dc, :], merged[:, dc, :], macc[:, 0, :], ALU.add), *(["merged_ready"] if b == 2 else []))
                    n += 1
            for t in range(NT):
                for k in range(2):
                    dve.wait_ge(sem("wo_psum"), 2 * t + k + 1)
                    done(tt(h[:, t, 512 * k:512 * k + 512], h[:, t, 512 * k:512 * k + 512], ps[:, 4 + k, :], ALU.add), "wo_used")
                if t < NT - 1:
                    done(v.memset(stat[:, 13:14], 0.0), "h_ready")
            done(v.memset(stat[:, 13:14], 0.0), "h_ready")
            done(v.memset(stat[:, 13:14], 0.0), "dve_phase")

            dve.wait_ge(sem("ss2_ready"), NT)
            done(ts(stat[:, 0:4], stat[:, 0:4], 1.0 / D, EPS, ALU.mult, ALU.add), "ms2_ready")
            dve.wait_ge(sem("rstd2_ready"), 1)
            dve.wait_ge(sem("g2_in"), 16)
            for t in range(NT):
                done(stt(n2[:, t, :], h[:, t, :], stat[:, t:t + 1], g2b[:], ALU.mult, ALU.mult), "n2_ready")
            NGE = NG + NE
            R = lambda i, w=NE: rt[:, i, 0:NT * w].rearrange("p (t e) -> p t e", t=NT)
            row3 = lambda z, w: z.rearrange("p (t a) -> p t a", a=1).broadcast_to([P, NT, w])
            rep = lambda z, w: z.rearrange("p (a e) -> p a e", a=1).broadcast_to([P, NT, w])
            dve.wait_ge(sem("lg_psum"), 1)
            lg_ps = ps[:, 2, 0:NT * NGE].rearrange("p (t e) -> p t e", t=NT)
            lg, le = R(0, NG), R(3)
            done(tt(lg, lg_ps[:, :, 0:NG], rep(rbias[:, 0:NG], NG), ALU.add))
            done(tt(le, lg_ps[:, :, NG:], rep(rbias[:, NG:], NE), ALU.add))
            gmax = rt[:, 4, 0:NT]

            def first(onehot, vals, mx, w, tmp):
                done(tt(onehot, vals, row3(mx, w), ALU.is_equal))
                done(ts(onehot, onehot, -1000.0, 1000.0, ALU.mult, ALU.add))
                done(tt(onehot, onehot, rep(iota_row[:, 0:w], w), ALU.add))
                done(v.tensor_reduce(tmp, onehot, AX, ALU.min))
                done(tt(onehot, rep(iota_row[:, 0:w], w), row3(tmp, w), ALU.is_equal))

            done(v.tensor_reduce(gmax, lg, AX, ALU.max))
            og = R(5, NG)
            first(og, lg, gmax, NG, rt[:, 6, 0:NT])
            done(tt(R(1, NG), lg, row3(gmax, NG), ALU.subtract))
            done(ts(og, og, 1.0, -NEG, ALU.subtract, ALU.mult))
            le4 = le.rearrange("p t (g e) -> p (t g) e", g=NG)
            done(ts(rt[:, 7, 0:NT * NG], rt[:, 5, 0:NT * NG], -1.0 / -NEG, None, ALU.mult))
            done(tt(le4, le4, rt[:, 5, 0:NT * NG].rearrange("p (t a) -> p t a", a=1).broadcast_to([P, NT * NG, EPG]), ALU.add))
            m1, m2 = rt[:, 8, 0:NT], rt[:, 9, 0:NT]
            oh1, oh2 = R(10), R(11)
            done(v.tensor_reduce(m1, le, AX, ALU.max))
            first(oh1, le, m1, NE, rt[:, 6, 0:NT])
            done(stt(le, oh1, 4 * NEG, le, ALU.mult, ALU.add))
            done(v.tensor_reduce(m2, le, AX, ALU.max))
            first(oh2, le, m2, NE, rt[:, 6, 0:NT])
            done(tt(rt[:, 2, 0:NT], m2, m1, ALU.subtract), "lg_ready")
            done(tt(R(12), oh1, oh2, ALU.add), "assign_ready")
            dve.wait_ge(sem("pe_exp"), 1)
            den, c1, c2 = rt[:, 6, 0:NT], rt[:, 13, 0:NT], rt[:, 13, NT:2 * NT]
            done(v.tensor_reduce(den, R(1, NG), AX, ALU.add))
            done(ts(c1, rt[:, 2, 0:NT], 1.0, None, ALU.add))
            done(tt(c1, c1, den, ALU.mult))
            done(v.reciprocal(c1, c1))
            done(tt(c2, c1, rt[:, 2, 0:NT], ALU.mult))
            dve.wait_ge(sem("rank_psum"), 1)
            rank = R(0)
            done(v.tensor_copy(rank, ps[:, 3, 0:NT * NE].rearrange("p (t e) -> p t e", t=NT)))
            cnt0 = rt[:, 4, NT:NT + NE]
            done(v.tensor_copy(cnt0, ps[:, 3, NT * NE:(NT + 1) * NE]), "counts_out")
            raw = R(7)
            done(v.tensor_copy(raw, rank))
            done(stt(rank, rank, 1.0, R(12), ALU.add, ALU.mult))
            done(ts(rank, rank, -1.0, None, ALU.add))
            def index(t, s, sel):
                v.tensor_tensor(Pm[:], sel, iota_f[:].rearrange("p (a n) -> p a n", a=1).broadcast_to([P, NT, P]),
                                ALU.is_equal).then_inc(sem("pm_ready"), 1)
                dve.wait_ge(sem("idx_psum"), t + 1)
                v.tensor_copy(idx[:, s:s + 1], ps[:, 7, 0:1]).then_inc(sem("idx_ready"), 1)

            def gated(t, s, bank):
                dve.wait_ge(sem("silu_ready"), t + 1)
                v.tensor_tensor(hg[:, s, 0:DE], hg[:, s, 0:DE], ps[:, bank, DE:], ALU.mult).then_inc(sem("hg_ready"), 1)

            def y_high(t, s, stores):
                dve.wait_ge(sem("down_psum"), t + 1)
                if stores is not None:
                    dve.wait_ge(sem(f"y_out{s}"), stores)
                v.tensor_copy(yo[:, s, 512:], ps[:, 5, :]).then_inc(sem("y_high"), 1)

            def tables():
                cnt, ov, inc, exc = (rt[:, 14, i * NE:(i + 1) * NE] for i in range(4))
                done(v.tensor_copy(cnt, cnt0))
                done(ts(ov, cnt, float(P) + 0.5, None, ALU.is_gt))
                for m in (2, 3):
                    done(stt(ov, cnt, m * float(P) + 0.5, ov, ALU.is_gt, ALU.add))
                done(v.tensor_tensor_scan(inc, ones[:, 0:NE], ov, 0.0, ALU.mult, ALU.add))
                done(tt(exc, inc, ov, ALU.subtract))
                base1, base2 = rt[:, 15, 0:NE], rt[:, 15, NE:2 * NE]
                done(ts(base1, iota_row[:], float(P), None, ALU.mult))
                done(ts(base2, exc, float(NE - 1), float(P), ALU.add, ALU.mult))
                done(tt(base2, base2, base1, ALU.subtract))
                over = R(3)
                done(ts(over, raw, float(P) - 0.5, None, ALU.is_gt))
                done(tt(over, over, rep(base2, NE), ALU.mult))
                done(tt(over, over, raw, ALU.add))
                done(tt(over, over, rep(base1, NE), ALU.add))
                for j, oh in enumerate((oh1, oh2)):
                    done(tt(oh, oh, over, ALU.mult))
                    done(v.tensor_reduce(rt[:, 15, 2 * NE + j * NT:2 * NE + (j + 1) * NT], oh, AX, ALU.add))
                    done(v.tensor_copy(rows[:].rearrange("p (t j) -> p j t", j=2)[:, j, :], rt[:, 15, 2 * NE + j * NT:2 * NE + (j + 1) * NT]))
                mk = rt[:, 9, 0:NE]
                done(v.memset(ovf[:], 0.0))
                done(v.tensor_copy(ovf[:, 0:1], inc[:, NE - 1:NE]))
                for k in range(NOV):
                    done(ts(mk, inc, k + 0.5, None, ALU.is_lt))
                    done(v.tensor_reduce(ovf[:, 1 + k:2 + k], mk, AX, ALU.add))
                    done(tt(mk, mk, ov, ALU.mult))
                    done(v.tensor_reduce(ovf[:, 1 + NOV + k:2 + NOV + k], mk, AX, ALU.add))
                    done(ts(ovf[:, 1 + NOV + k:2 + NOV + k], ovf[:, 1 + NOV + k:2 + NOV + k], -float(P), (k + 1) * float(P), ALU.mult, ALU.add))
                done(v.tensor_copy(ovi[:], ovf[:]), "ov_ready")

            def sel_of(e):
                return rank[:, :, e:e + 1].broadcast_to([P, NT, P])
            for t in range(-2, NE + 1):
                if t + 2 < NE:
                    if t >= 0:
                        dve.wait_ge(sem(f"xg_in{t % 2}"), 16 * (t // 2 + 1))
                    if t >= -1:
                        dve.wait_ge(sem("idx_psum"), t + 2)
                    index(t + 2, t % 2, sel_of(t + 2))
                if t == -1:
                    tables()
                if 0 <= t < NE:
                    gated(t, t % 2, 2 + 4 * (t % 2))
                if t >= 1:
                    y_high(t - 1, (t - 1) % 2, 16 * ((t - 1) // 2) if t >= 3 else None)
            n_ov = dve.value_load(ovi[0:1, 0:1], min_val=0, max_val=NOV)
            with dve.Fori(0, NOV) as k:
                with dve.If(k < n_ov):
                    e = dve.value_load(ovi[0:1, bass.ds(k + 1, 1)], min_val=0, max_val=NE - 1)
                    ov_rank = rt[:, 8, 0:NT]
                    dve.wait_ge(sem("down_psum"), k + NE)
                    v.tensor_scalar(ov_rank, rank[:, :, bass.ds(e, 1)].rearrange("p t e -> p (t e)"), ovf[:, bass.ds(k + NOV + 1, 1)], None,
                                    ALU.subtract).then_inc(sem("ov_rank"), 1)
                    dve.wait_ge(sem("ov_rank"), k + 1)
                    index(k + NE, 0, ov_rank.rearrange("p (t a) -> p t a", a=1).broadcast_to([P, NT, P]))
                    gated(k + NE, 0, 2)
                    dve.wait_ge(sem("y_out0"), k * 16 + NE * 8)
                    y_high(k + NE, 0, None)
            for t in range(NT):
                for j, cc in ((0, c1), (1, c2)):
                    dve.wait_ge(sem(f"ysel_in{j}"), 16 * (t + 1))
                    ins = stt(h[:, t, :], ysel[:, j, :], cc[:, t:t + 1], h[:, t, :], ALU.mult, ALU.add)
                    done(ins, "ysel_used")
                done(v.memset(stat[:, 13:14], 0.0), "out_ready")

        @block.tensor
        def _(pe):
            mm = nc.tensor.matmul
            tr = nc.tensor.transpose
            pe.wait_ge(sem("ident_ready"), 1)
            pe.wait_ge(sem("xs_ready"), NT + 1)
            for c in range(DC):
                if c >= 4:
                    pe.wait_ge(sem("nT_ready"), c - 3)
                for t in range(NT):
                    ins = tr(ps[:, c % 4, t * P:(t + 1) * P], xs[:, t, c * P:(c + 1) * P], ident[:])
                ins.then_inc(sem("xT_psum"), 1)
            for c in range(DC):
                ins = tr(ps[:, 4, c * META:(c + 1) * META], metax[0:META, c * P:(c + 1) * P], ident[0:META, 0:META])
            ins.then_inc(sem("xT_psum"), 1)
            pe.wait_ge(sem("nT_ready"), DC)
            pe.wait_ge(sem("nT_meta"), 1)
            n = 0
            for i, (kind, cols) in enumerate(pieces):
                pe.wait_ge(sem(f"ring{i % RING}"), landed[i])
                w = slot(i)
                if kind in "sq":
                    for j in range(2):
                        if n >= 2:
                            pe.wait_ge(sem("chunk_out"), n - 1)
                        o = 2 * (n % 2)
                        for hf in range(2):
                            for c in range(DC):
                                ins = mm(ps[:, o + hf, 0:HALF], w[:, c, j * P:(j + 1) * P], nT[:, c, hf * HALF:(hf + 1) * HALF],
                                         start=(c == 0), stop=(c == DC - 1))
                        ins.then_inc(sem("chunk_psum"), 1)
                        n += 1
                else:
                    nw = cols[0][1]
                    for k0, r in KT:
                        pe.wait_ge(sem("chunk_out"), n - 1 if n < SC + 12 else n - 3)
                        for c in range(DC):
                            ins = mm(ps[0:r, n % 4, 0:nw], nT[:, c, k0:k0 + r], w[:, c, 0:nw], start=(c == 0), stop=(c == DC - 1))
                        ins.then_inc(sem("chunk_psum"), 1)
                        n += 1
                pe.wait_ge(sem("chunk_psum"), n)
                pe.sem_inc(sem("piece_used"), 1)
            pe.wait_ge(sem("consts_ready"), 1)
            for m in range(6):
                pe.wait_ge(sem("fsq_ready"), m + 1)
                if m >= 2:
                    pe.wait_ge(sem("norm_used"), m - 1)
                for hf in range(2):
                    ins = mm(ps[:, 4 * (m % 2) + hf, 0:HALF], head_ones[:], tmp_shift[:, 0, hf * HALF:(hf + 1) * HALF], start=True, stop=True)
                ins.then_inc(sem("norm_psum"), 1)
            pe.wait_ge(sem("norm_psum"), 6)
            pe.sem_inc(sem("pe_phase"), 1)

            pe.wait_ge(sem("dve_phase"), 1)
            pe.wait_ge(sem("act_phase"), 1)
            pe.wait_ge(sem("wd_ready"), 1)
            for c in range(RC):
                for q in range(2):
                    if c >= 1:
                        pe.wait_ge(sem("wa_used"), 2 * (c - 1) + q + 1)
                    rs = slice(64 * q, 64 * q + 64)
                    for hf in range(2):
                        ins = mm(ps[:, 2 * q + hf, 0:HALF], up_w[rs, c * P:(c + 1) * P], U[rs, 9, 1 + hf * HALF:1 + (hf + 1) * HALF], start=True, stop=True)
                    ins.then_inc(sem("wa_psum"), 1)
            for c in range(RC):
                pe.wait_ge(sem("kk_sq"), c + 1)
                if c >= 1:
                    pe.wait_ge(sem("kk_used"), c)
                for hf in range(2):
                    ins = mm(ps[:, 4 + hf, 0:HALF], head_ones[:], Bt[:, c, hf * HALF:(hf + 1) * HALF], start=True, stop=True)
                ins.then_inc(sem("kk_psum"), 1)
            pe.wait_ge(sem("kk_used"), RC)
            for c in range(RC):
                pe.wait_ge(sem("rk_ready"), c + 1)
                if c >= 1:
                    pe.wait_ge(sem("bonus_used"), c)
                for hf in range(2):
                    ins = mm(ps[:, 4 + hf, 0:HALF], head_ones[:], tb[:, c, hf * HALF:(hf + 1) * HALF], start=True, stop=True)
                ins.then_inc(sem("bonus_psum"), 1)
            pe.wait_ge(sem("bonus_used"), RC)
            pe.wait_ge(sem("tilde_ready"), 1)
            quads = [slice(0, 64), slice(64, 128)]

            def units(bank, lhs, rhs, acc=None, c0=0, c1=NCH):
                for c in range(c0, c1):
                    for q in quads:
                        ins = mm(psf[q, 512 * bank + c * CH:512 * bank + (c + 1) * CH], lhs(q, c), rhs(q, c), start=True, stop=True)
                return ins
            for p in range(RC):
                cm = lambda z: (lambda q, c: z[q, p, c * CH:(c + 1) * CH])
                um = lambda z: (lambda q, c: z[q, c, :])
                idq = lambda q, c: ident2[q, :]
                vsrc = lambda q, c: U[q, 6 + p, 1 + c * CH:1 + min((c + 1) * CH, L)]
                if p >= 1:
                    pe.wait_ge(sem("w1_ready"), p)
                    pe.wait_ge(sem("akv_ready"), p)
                for k, z in enumerate((At, Bt, Kt)):
                    if k == 2:
                        pe.wait_ge(sem("tr_used"), 4 * p + 1)
                    units(2 * (k % 2), cm(z), idq).then_inc(sem("tr_psum"), 1)
                pe.wait_ge(sem("tr_used"), 4 * p + 2)
                units(2, vsrc, idq, c1=NCH - 1)
                w = L - (NCH - 1) * CH
                for q in quads:
                    ins = mm(psf[q, 1024 + (NCH - 1) * CH:1024 + NCH * CH], At[q, p, LP - CH:LP], ident2[q, :], start=True, stop=True)
                for q in quads:
                    ins = mm(psf[q.start:q.start + w, 1024 + (NCH - 1) * CH:1024 + NCH * CH], vsrc(q, NCH - 1), ident2[q, :], start=True, stop=True)
                ins.then_inc(sem("tr_psum"), 1)
                for k, (lhs, rhs) in enumerate(((Kt, At), (Kt, Rt), (Bt, At), (Bt, Rt), (At, Bt))):
                    if k >= 2:
                        pe.wait_ge(sem("g_used"), 5 * p + k - 1)
                    if k < 2 and p >= 1:
                        pe.wait_ge(sem("w2_ready"), p)
                        pe.wait_ge(sem("y_out_rwkv"), NCH * p)
                    units(4 + 2 * (k % 2), cm(lhs), cm(rhs)).then_inc(sem("g_psum"), 1)
                pe.wait_ge(sem("g_used"), 5 * p + 5)
                pe.wait_ge(sem("tr_used"), 4 * p + 4)
                for lv in range(1, 6):
                    pe.wait_ge(sem("T_ready"), 6 * p + lv)
                    units(4, um(NTm), um(Tm)).then_inc(sem("H_psum"), 1)
                    pe.wait_ge(sem("H_ready"), 5 * p + lv)
                    if lv < 5:
                        units(6, um(TTm), um(Hm)).then_inc(sem("G_psum"), 1)
                    units(0, um(Hm), um(TTm)).then_inc(sem("G_psum"), 1)
                pe.wait_ge(sem("T_ready"), 6 * p + 6)
                units(0, um(AtT), um(TTm)).then_inc(sem("w1_psum"), 1)
                units(2, um(AKT), um(VT)).then_inc(sem("akv_psum"), 1)
                pe.wait_ge(sem("akv_ready"), p + 1)
                units(4, um(TTm), um(Hm)).then_inc(sem("w2_psum"), 1)
                pe.wait_ge(sem("w1_ready"), p + 1)
                pe.wait_ge(sem("w2_ready"), p + 1)
                for c in range(NCH):
                    pe.wait_ge(sem("S_ready"), NCH * p + c + 1)
                    for q in quads:
                        ins = mm(ps[q, 6, 0:CH], W1T[q, c, :], Ssb[q, :], start=True, stop=True)
                    ins.then_inc(sem("u_psum"), 1)
                    if c >= 2:
                        pe.wait_ge(sem("y_out_rwkv"), NCH * p + c - 1)
                    yq = lambda q: ps[q, 5 + 2 * (c % 2), 0:CH]
                    for q in quads:
                        mm(yq(q), Ssb[q, :], Rt[q, p, c * CH:(c + 1) * CH], start=True, stop=False)
                        mm(yq(q), VT[q, c, :], RKT[q, c, :], start=False, stop=False)
                        if c < NCH - 1:
                            pass
                    pe.wait_ge(sem("U_ready"), NCH * p + c + 1)
                    if c < NCH - 1:
                        for q in quads:
                            mm(ps[q, 6, 128:128 + CH], KtT[q, c, :], VT[q, c, :], start=True, stop=False)
                            ins = mm(ps[q, 6, 128:128 + CH], BtT[q, c, :], Usb[q, :], start=False, stop=True)
                        ins.then_inc(sem("s_psum"), 1)
                    for q in quads:
                        ins = mm(yq(q), Usb[q, :], RBT[q, c, :], start=False, stop=True)
                    ins.then_inc(sem("y_psum"), 1)
            pe.wait_ge(sem("act_phase"), 2)
            for c in range(RC):
                if c >= 1:
                    pe.wait_ge(sem("ln_used"), c)
                for q, z in enumerate((ta, tb)):
                    for hf in range(2):
                        ins = mm(ps[:, 2 * q + hf, 0:HALF], head_ones[:], z[:, c, hf * HALF:(hf + 1) * HALF], start=True, stop=True)
                    ins.then_inc(sem("ln_psum"), 1)
            pe.wait_ge(sem("ln_psum"), 2 * RC)
            pe.sem_inc(sem("pe_phase"), 1)

            pe.wait_ge(sem("dve_phase"), 2)
            pe.wait_ge(sem("f_ready"), 1)
            for hf in range(2):
                lo, hi = hf * HALF, (hf + 1) * HALF
                tiles = [(i, k0, r) for i, (k0, r) in enumerate(KT) if k0 < hi]
                for i, k0, r in tiles:
                    d0, d1 = max(lo, k0), min(hi, k0 + r)
                    first_ = i == 0
                    last_ = i == tiles[-1][0]
                    if first_ and lo == 0:
                        mm(ps[0:FH, hf, 0:P], flog[0:r, i, :], tri_le[0:r, 0:P], start=True, stop=False, skip_group_check=True)
                    elif d0 < d1:
                        mm(ps[0:FH, hf, d0 - lo:d1 - lo], flog[0:r, i, :], tri_le[0:r, d0 - k0:d1 - k0], start=False, stop=False, skip_group_check=True)
                    e0 = max(lo, k0 + r)
                    while e0 < hi:
                        e1 = min(hi, e0 + P)
                        ins = mm(ps[0:FH, hf, e0 - lo:e1 - lo], flog[0:r, i, :], ones[0:r, 0:e1 - e0],
                                 start=(i == 0 and e0 == lo), stop=False, skip_group_check=True)
                        e0 = e1
                    if d0 < d1 and last_:
                        pass
            ins = mm(ps[0:FH, 6, 0:1], ones[0:2, 0:FH], ones[0:2, 0:1], start=True, stop=True)
            ins.then_inc(sem("fcum_psum"), 1)
            pe.wait_ge(sem("fcum_ready"), 2)
            for hh in range(SH):
                cq, bq = qchunk("sb", hh, 0)
                ck, bk = qchunk("sb", hh, 1)
                q64 = slice(bq, bq + 64)
                if hh >= 1:
                    pe.wait_ge(sem("A_ready"), 5 * hh)
                for i, (k0, r) in enumerate(KT):
                    n = min(SEQ, L - k0)
                    ins = mm(ps[0:r, i, 0:n], QK[q64, ck, k0:k0 + r], QK[q64, cq, L - n:L], start=True, stop=False, skip_group_check=True)
                    ins.then_inc(sem("z_psum"), 1)
                pe.wait_ge(sem("sp_ready"), 5 * hh + 5)
                for i, (k0, r) in enumerate(KT):
                    n = min(SEQ, L - k0)
                    q0 = META if i == 0 else 0
                    mm(ps[0:r, i, 0:n], tri_sb[0:r, 0:r], s_b[0:r, i, 0:n], start=False, stop=False, skip_group_check=True)
                    for i2 in range(i + 1, 5):
                        k2, r2 = KT[i2]
                        n2_ = L - k2
                        mm(ps[0:r, i, n - n2_:n], neg_ones[0:r2, 0:r], s_b[0:r2, i2, 0:n2_], start=False, stop=False, skip_group_check=True)
                    w = r - q0
                    mm(ps[0:r, i, 0:w], ident[0:r, 0:r], neg_sb[0:r, q0:q0 + w], start=False, stop=True, skip_group_check=True).then_inc(sem("w_psum"), 1)
                row = 64 * (hh % 2) if hh < 4 else 0
                o = ps[row:row + 64, 6, :]
                for i, (k0, r) in enumerate(KT):
                    n = min(SEQ, L - k0)
                    pe.wait_ge(sem("A_ready"), 5 * hh + i + 1)
                    if i == 0 and hh >= 1:
                        pe.wait_ge(sem("sb_used"), hh)
                    ins = mm(o[:, SEQ - n:], V[0:r, i, hh * HD:(hh + 1) * HD], s_c[0:r, i, 0:n], start=(i == 0), stop=(i == 4), skip_group_check=True)
                ins.then_inc(sem("o_psum"), 1)
            pe.wait_ge(sem("o_psum"), SH)
            pe.sem_inc(sem("pe_phase"), 1)

            pe.wait_ge(sem("dve_phase"), 3)
            pe.wait_ge(sem("act_phase"), 3)
            pe.wait_ge(sem("frows"), 32 * FH)
            def scores(u):
                hh, i = u // NT, u % NT
                cq, bq = qchunk("fox", hh, 0)
                ck, _ = qchunk("fox", hh, 1)
                q64 = slice(bq, bq + 64)
                kn = META + P * (i + 1)
                qs = slice(META + i * P, META + (i + 1) * P)
                if u >= 2:
                    pe.wait_ge(sem("p_ready"), u - 1)
                for k0 in range(0, kn, 512):
                    k1 = min(kn, k0 + 512)
                    b = 2 * (u % 2) + k0 // 512
                    o = ps[:, b, 0:k1 - k0]
                    mm(o, QK[q64, cq, qs], QK[q64, ck, k0:k1], start=True, stop=False, skip_group_check=True)
                    mm(o, FL[0:2, hh, qs], FR[0:2, hh, k0:k1], start=False, stop=False, skip_group_check=True)
                    d0, d1 = max(k0, kn - P), k1
                    ins = mm(o[:, d0 - k0:d1 - k0], ident[:], neg_fox[:, d0 - (kn - P):d1 - (kn - P)], start=False, stop=True, skip_group_check=True)
                ins.then_inc(sem("s_ready"), 1)
            NU = FH * NT
            scores(0)
            for u in range(NU):
                hh, i = u // NT, u % NT
                if u + 1 < NU:
                    scores(u + 1)
                pe.wait_ge(sem("pn_ready"), u + 1)
                if u >= 1:
                    pe.wait_ge(sem("pTs_ready"), u)
                for k in range(i + 1):
                    tr(ps[:, 4, k * P:(k + 1) * P], p_f[:, u % 2, k * P:(k + 1) * P], ident[:])
                tr(ps[0:16, 5, 0:P], p_f[:, u % 2, (i + 1) * P:(i + 1) * P + 16], ident[:]).then_inc(sem("pT_psum"), 1)
                pe.wait_ge(sem("pTs_ready"), u + 1)
                if u >= 1:
                    pe.wait_ge(sem("of_used"), u)
                row = 64 * (hh % 2) if hh < 4 else 64
                o = ps[row:row + 64, 6, 0:P]
                vs = slice(SW + hh * HD, SW + (hh + 1) * HD)
                for k in range(i + 1):
                    mm(o, V[:, k, vs], pT[:, u % 2, k, :], start=(k == 0), stop=False)
                mm(o, V[0:16, i + 1, vs], pT[0:16, u % 2, i + 1, :], start=False, stop=True).then_inc(sem("of_psum"), 1)
            pe.wait_ge(sem("of_psum"), NU)
            pe.sem_inc(sem("pe_phase"), 1)

            pe.wait_ge(sem("dve_phase"), 4)
            pe.wait_ge(sem("act_phase"), 4)
            n = 0
            for dc in range(DC):
                pe.wait_ge(sem(f"proj_w{dc % 2}"), 16 * 8 * (dc // 2 + 1))
                for b in range(3):
                    if n >= 2:
                        pe.wait_ge(sem("gsig_ready"), n - 1)
                        pe.wait_ge(sem("gsig_used"), n - 1)
                    for c in range(DC):
                        ins = mm(ps[:, n % 2, :], wgr[:, dc % 2, b * DC + c, :], nT[:, c, META:L], start=(c == 0), stop=(c == DC - 1))
                    ins.then_inc(sem("gate_psum"), 1)
                    for c in range(3):
                        rs = slice(0, P) if b == 0 or c < 2 else slice(64 * (b - 1), 64 * b)
                        ins = mm(ps[:, 2 + n % 2, :], wpr[rs, dc % 2, 3 * b + c, :], yT[b][rs, c, :], start=(c == 0), stop=(c == 2))
                    ins.then_inc(sem("proj_psum"), 1)
                    n += 1
                pe.wait_ge(sem("proj_psum"), n)
                pe.sem_inc(sem("proj_used"), 1)
            pe.wait_ge(sem("merged_ready"), DC)
            pe.wait_ge(sem("wout_in"), 16)
            for t in range(NT):
                for k in range(2):
                    if t >= 1:
                        pe.wait_ge(sem("wo_used"), 2 * (t - 1) + k + 1)
                    for c in range(DC):
                        ins = mm(ps[:, 4 + k, :], merged[:, c, t * P:(t + 1) * P], wout[:, c, k * 512:(k + 1) * 512], start=(c == 0), stop=(c == DC - 1))
                    ins.then_inc(sem("wo_psum"), 1)
            pe.wait_ge(sem("wo_psum"), 2 * NT)
            pe.sem_inc(sem("pe_phase"), 1)

            pe.wait_ge(sem("dve_phase"), 5)
            pe.wait_ge(sem("act_phase"), 5)
            pe.wait_ge(sem("n2_ready"), NT)
            for c in range(DC):
                if c >= 2:
                    pe.wait_ge(sem("n2T_ready"), c - 1)
                for t in range(NT):
                    ins = tr(ps[:, c % 2, t * P:(t + 1) * P], n2[:, t, c * P:(c + 1) * P], ident[:])
                ins.then_inc(sem("n2T_psum"), 1)
            pe.wait_ge(sem("n2T_ready"), DC)
            for t in range(NT):
                for c in range(DC):
                    ins = mm(ps[:, 2, t * (NG + NE):(t + 1) * (NG + NE)], n2T[:, c, t * P:(t + 1) * P], rw[:, c, :], start=(c == 0), stop=(c == DC - 1))
            ins.then_inc(sem("lg_psum"), 1)
            pe.wait_ge(sem("assign_ready"), 1)
            asg = rt[:, 12, :].rearrange("p (t e) -> p t e", t=NT)
            for t in range(NT):
                for t2 in range(t):
                    mm(ps[:, 3, t * NE:(t + 1) * NE], ones[:], asg[:, t2, :], start=(t2 == 0), stop=False)
                mm(ps[:, 3, t * NE:(t + 1) * NE], tri_lt[:], asg[:, t, :], start=(t == 0), stop=True)
            for t in range(NT):
                ins = mm(ps[:, 3, NT * NE:(NT + 1) * NE], ones[:], asg[:, t, :], start=(t == 0), stop=(t == NT - 1))
            ins.then_inc(sem("rank_psum"), 1)

            def index(t):
                for k in range(NT):
                    ins = mm(ps[:, 7, 0:1], Pm[:, k, :], tokid[:, k:k + 1], start=(k == 0), stop=(k == NT - 1))
                ins.then_inc(sem("idx_psum"), 1)

            def rows_T(t, s, landed_):
                pe.wait_ge(sem(f"xg_in{s}"), landed_)
                for k in range(2):
                    for c in range(4):
                        ins = tr(ps[:, k, c * P:(c + 1) * P], xg[:, s, (4 * k + c) * P:(4 * k + c + 1) * P], ident[:])
                    ins.then_inc(sem("xgT_psum"), 1)

            def gate_up(t, s, bank, landed_):
                pe.wait_ge(sem("xgT_ready"), t * 2 + 2)
                pe.wait_ge(sem(f"moe_w{s}"), landed_)
                for c in range(DC):
                    ins = mm(ps[:, bank, :], xgT[:, s, c, :], w1[:, s, c, :], start=(c == 0), stop=(c == DC - 1))
                ins.then_inc(sem("gu_psum"), 1)

            def hidden_T(t, s):
                pe.wait_ge(sem("hg_ready"), t + 1)
                for c in range(2):
                    ins = tr(ps[:, 3, c * P:(c + 1) * P], hg[:, s, c * P:(c + 1) * P], ident[:])
                ins.then_inc(sem("hT_psum"), 1)

            def down(t, s, landed_):
                pe.wait_ge(sem("hT_ready"), t + 1)
                pe.wait_ge(sem(f"moe_d{s}"), landed_)
                for k in range(2):
                    for c in range(2):
                        ins = mm(ps[:, 4 + k, :], hT[:, s, c, :], w2[:, s, c, 512 * k:512 * k + 512], start=(c == 0), stop=(c == 1))
                ins.then_inc(sem("down_psum"), 1)

            pe.wait_ge(sem("pm_ready"), 1)
            index(0)
            pe.wait_ge(sem("pm_ready"), 2)
            pe.wait_ge(sem("idx_ready"), 1)
            index(1)
            rows_T(0, 0, 16)
            for t in range(NE + 1):
                if t < NE:
                    if t >= 2:
                        pe.wait_ge(sem("hg_ready"), t - 1)
                    gate_up(t, t % 2, 2 + 4 * (t % 2), 32 * (t // 2 + 1))
                if t >= 1:
                    if t >= 2:
                        pe.wait_ge(sem("hT_ready"), t - 1)
                    hidden_T(t - 1, (t - 1) % 2)
                if t + 1 < NE:
                    pe.wait_ge(sem("xgT_ready"), 2 * t + 2)
                    rows_T(t + 1, (t + 1) % 2, 16 * ((t + 1) // 2 + 1))
                if t + 2 < NE:
                    pe.wait_ge(sem("pm_ready"), t + 3)
                    pe.wait_ge(sem("idx_ready"), t + 2)
                    index(t + 2)
                if t >= 1:
                    if t >= 2:
                        pe.wait_ge(sem("y_low"), t - 1)
                        pe.wait_ge(sem("y_high"), t - 1)
                    down(t - 1, (t - 1) % 2, 16 * ((t - 1) // 2 + 1))
            pe.wait_ge(sem("ov_ready"), 1)
            n_ov = pe.value_load(ovi[0:1, 0:1], min_val=0, max_val=NOV)
            with pe.Fori(0, NOV) as k:
                with pe.If(k < n_ov):
                    t = k + NE
                    pe.wait_ge(sem("pm_ready"), k + NE + 1)
                    pe.wait_ge(sem("y_low"), k + NE)
                    pe.wait_ge(sem("y_high"), k + NE)
                    index(t)
                    rows_T(t, 0, k * 16 + 16 * (NE // 2 + 1))
                    gate_up(t, 0, 2, k * 32 + 32 * (NE // 2 + 1))
                    hidden_T(t, 0)
                    down(t, 0, k * 16 + 16 * (NE // 2 + 1))


_INS = ["x", "meta_tokens", "norm1_g", "w_in", "rwkv_mu", "rwkv_w_up", "rwkv_w0", "rwkv_a_up", "rwkv_a0",
        "rwkv_k_k", "rwkv_k_a", "rwkv_r_k", "rwkv_ln_g", "rwkv_ln_b", "fox_f_b", "fox_q_g", "fox_k_g",
        "w_p_rwkv", "w_p_sb", "w_p_fox", "w_out", "norm2_g", "moe_wg", "moe_bg", "moe_we", "moe_be",
        "moe_w_gate", "moe_w_up", "moe_w_down"]


def kernel(**inputs):
    import numpy as _np
    import concourse.bacc as _bacc
    from concourse import mybir as _mybir
    from concourse.bass_utils import run_bass_kernel_spmd as _run

    nc = _bacc.Bacc("TRN2", target_bir_lowering=False, num_devices=1)
    arrays, args = {}, []
    for name in _INS:
        a = _np.ascontiguousarray(inputs[name])
        if name != "meta_tokens":
            a = a[0]
        arrays["in_" + name] = a
        args.append(nc.dram_tensor("in_" + name, a.shape, _mybir.dt.from_np(a.dtype), kind="ExternalInput").ap())
    o = nc.dram_tensor("out_0", (SEQ, D), _mybir.dt.float32, kind="ExternalOutput").ap()
    hybrid_layer(nc, *args, o)
    r = _run(nc, [arrays], core_ids=[0])
    return r.results[0]["out_0"].reshape(1, SEQ, D)
```

```python
from contextlib import ExitStack

import concourse.bass as bass
from concourse import mybir

F32 = mybir.dt.float32
U32 = mybir.dt.uint32
I32 = mybir.dt.int32
ALU = mybir.AluOpType
ACT = mybir.ActivationFunctionType
AX = mybir.AxisListType.X

P = 128
D = 1024
DC = D // P
META = 16
SEQ = 512
L = META + SEQ
HALF = L // 2
NT = SEQ // P
HD = 64
RH, SH, FH = 6, 5, 5
RW, SW, FW = RH * HD, SH * HD, FH * HD
RC = RW // P
SHIFT_W = 3 * RW + 2 * HD
SC = SHIFT_W // P
C_SBQ = SHIFT_W
C_SBK = C_SBQ + SW
C_SBV = C_SBK + SW
C_FQ = C_SBV + SW
C_FK = C_FQ + FW
C_FV = C_FK + FW
C_F = C_FV + FW
C_G = C_F + FH
PIECE = 256
RING = 3
RING_W = FW + FH
CH = 64
NCH = -(-L // CH)
LP = NCH * CH
NG, EPG = 4, 4
NE = NG * EPG
DE = 256
EPS = 1e-6
LN_EPS = 64e-5
DECAY = 0.6065306597126334
NEG = -1e30
FOX_FILL = 2
EARLY_GATES = 3
NOV = SEQ * 2 // P - 1
KT = [(128 * i, min(128, L - 128 * i)) for i in range(5)]


def hybrid_layer(nc, x, meta, g1, w_in, mu, w_up, w0, a_up, a0, k_k, k_a, r_k, ln_g, ln_b, f_b, q_g, k_g,
                 wp_r, wp_s, wp_f, w_out, g2, wg, bg, we, be, m_gate, m_up, m_down, out):
    n2_dram = nc.dram_tensor("n2_rows", [SEQ, D], F32, kind="Internal").ap()
    y_dram = nc.dram_tensor("expert_rows", [(NE + NOV) * P, D], F32, kind="Internal").ap()

    with ExitStack() as ctx:
        def sb(name, shape, dt=F32):
            return ctx.enter_context(nc.sbuf_tensor(name, shape, dt))

        sems = {}

        def sem(name):
            if name not in sems:
                sems[name] = ctx.enter_context(nc.semaphore(name))
            return sems[name]

        ctx.enter_context(nc.allow_non_contiguous_dma("small parameter vectors"))
        ps = ctx.enter_context(nc.psum_tensor("ps", [P, 8, 512], F32))
        psf = ps[:].rearrange("p b n -> p (b n)")

        ident = sb("ident", [P, P])
        ones = sb("ones", [P, P])
        head_ones = sb("head_ones", [P, P])
        tri_le = sb("tri_le", [P, P])
        tri_lt = sb("tri_lt", [P, P])
        tri_sb = sb("tri_sb", [P, P])
        neg_sb = sb("neg_sb", [P, P])
        neg_fox = sb("neg_fox", [P, P])
        neg_ones = sb("neg_ones", [P, P])
        ident2 = sb("ident2", [P, CH])
        strict_st = sb("strict_st", [P, CH])
        strict_ts = sb("strict_ts", [P, CH])
        incl_st = sb("incl_st", [P, CH])
        lev_ts = sb("lev_ts", [P, 6, CH], U32)
        lev_st = sb("lev_st", [P, 6, CH], U32)
        reset = sb("reset", [P, L])
        chan = sb("chan", [P, 64])
        g1c, muc, w0c, a0c = chan[:, 0:8], chan[:, 8:18], chan[:, 18:21], chan[:, 21:24]
        kkc, kac, rkc = chan[:, 24:27], chan[:, 27:30], chan[:, 30:33]
        lgc, lbc = chan[:, 33:36], chan[:, 36:39]
        qgc, kgc, qg8 = chan[:, 39:40], chan[:, 40:41], chan[:, 41:42]
        up_w = sb("up_w", [P, RW])
        fb = sb("fb", [P, FH])
        rbias = sb("rbias", [P, NG + NE])
        rw = sb("rw", [P, DC, NG + NE])
        iota_f = sb("iota_f", [P, P])
        iota_row = sb("iota_row", [P, NE])
        tokid = sb("tokid", [P, NT])
        stat = sb("stat", [P, 16])
        h = sb("h", [P, NT, D])
        yT = [sb(f"yT{i}", [P, 3, SEQ]) for i in range(3)]
        ARENA = 40700
        arena = sb("arena", [P, ARENA])
        at = [0]

        def carve(shape, dt=F32, start=None):
            if start is not None:
                at[0] = start
            n = 1
            for s in shape:
                n *= s
            v = arena[:, at[0]:at[0] + n]
            at[0] += n
            assert at[0] <= ARENA, at[0]
            if len(shape) == 2:
                v = v.rearrange("p (a b) -> p a b", a=shape[0])
            if len(shape) == 3:
                v = v.rearrange("p (a b c) -> p a b c", a=shape[0], b=shape[1])
            return v

        U = carve([SC, L + 1])
        QK = carve([10, L])
        V = carve([5, 2 * SW])
        flog = carve([5, FH])
        nT = carve([DC, L])
        base = at[0]
        At = carve([RC, LP], start=base)
        Rt, Bt, Kt = carve([RC, LP]), carve([RC, LP]), carve([RC, LP])
        Pc = carve([RC, NCH * (CH + 1)])
        tc_ = carve([RC, L])
        ta = carve([RC, L])
        tb = carve([RC, L])
        un_at = at[0]
        un = [carve([NCH, CH]) for _ in range(12)]
        AtT, BtT, KtT, VT, NTm, Nm, AKT, RBT, RKT, Tm, TTm, Hm = un
        W1T = carve([NCH, CH])
        W2 = carve([NCH, CH])
        Ssb = carve([CH])
        Usb = carve([CH])
        tmp_shift = carve([2, L])
        ring = carve([RING, DC * RING_W], start=un_at)
        assert at[0] <= un_at + 14 * NCH * CH
        xs = carve([NT, D], start=base)
        metax = carve([D])
        late = [arena[:, 0:DC * RING_W], arena[:, base + 4 * RC * LP + RC * NCH * (CH + 1) + RC * L:][:, 0:DC * RING_W]]
        mask_tmp = yT[0][:, 0, 0:6 * CH].rearrange("p (a b) -> p a b", a=6)
        FL = carve([FH, L], start=base)
        FR = carve([FH, L])
        fcum = carve([L])
        s_a = carve([2, SEQ])
        key_tile = carve([2 * sum(min(SEQ, L - k0) for k0, _ in KT)])
        starts = [sum(min(SEQ, L - k) for k, _ in KT[:i]) for i in range(6)]
        s_b = [key_tile[:, starts[i]:starts[i + 1]] for i in range(5)]
        s_c = [key_tile[:, starts[5] + starts[i]:starts[5] + starts[i + 1]] for i in range(5)]
        p_f = key_tile[:, 0:2 * L].rearrange("p (a b) -> p a b", a=2)
        pT = key_tile[:, 2 * L:2 * L + 2 * 5 * P].rearrange("p (a b c) -> p a b c", a=2, b=5)
        gate_w = carve([4, DC, P])
        assert base + 4 * RC * LP + RC * NCH * (CH + 1) + RC * L <= at[0] - 3 * DC * P and at[0] <= un_at + NCH * CH
        gates_hi = carve([14, SEQ])
        gates_lo = carve([10, SEQ], start=0)
        gate = lambda n: gates_lo[:, n, :] if n < 10 else gates_hi[:, n - 10, :]
        merged = carve([DC, SEQ], start=SC * (L + 1))
        macc = carve([SEQ])
        wpr = carve([2, 9, P])
        assert at[0] <= base - DC * L
        wout = carve([DC, D], start=base)
        w1 = carve([2, DC, 2 * DE], start=0)
        w2 = carve([2, 2, D])
        xg = carve([2, D])
        xgT = carve([2, DC, P])
        hg = carve([2, 2 * DE])
        hT = carve([2, 2, P])
        yo = carve([2, D])
        Pm = carve([NT, P])
        assert at[0] <= base + DC * D
        n2 = carve([NT, D], start=base + DC * D)
        n2T = carve([DC, SEQ])
        g2b = carve([D])
        rt = carve([16, NT * NE])
        ysel = carve([2, D])
        h_sq = carve([D])
        idx = sb("idx", [P, 4], U32)
        rows = sb("rows", [P, 2 * NT], U32)
        ovi = sb("ovi", [P, 2 * NOV + 2], I32)
        ovf = sb("ovf", [P, 2 * NOV + 2])

        wv = w_in.rearrange("(c p) n -> p c n", p=P)
        pieces = [("s", [(i * PIECE, PIECE)]) for i in range(SC // 2)]
        pieces += [("q", [(c, PIECE)]) for c in (C_SBQ, C_SBK, C_FQ, C_FK)]
        pieces += [("q", [(C_SBQ + 256, 64), (C_FQ + 256, 64), (C_SBK + 256, 64), (C_FK + 256, 64)])]
        pieces += [("v", [(C_SBV, SW)]), ("v", [(C_FV, FW + FH)])]
        N_SHIFT, N_RING = SC // 2, SC // 2 + 3
        landed = []
        for i, (_, cols) in enumerate(pieces):
            before = i - RING if i < N_RING else (i - 2 if i >= N_RING + 2 else -1)
            landed.append((landed[before] if before >= 0 else 0) + 16 * len(cols))

        def slot(i):
            z = ring[:, i % RING, :] if i < N_RING else late[(i - N_RING) % 2]
            return z.rearrange("p (c n) -> p c n", c=DC)

        def slot_sem(i):
            return sem(f"ring{i % RING}" if i < N_RING else f"late{(i - N_RING) % 2}")

        groups = [(N_SHIFT + f // 4, "q", f // 2, f % 2) for f in range(20)] + [(N_SHIFT + 5 + f // 5, "v", f // 5, f % 5) for f in range(10)]
        NF = len(groups)
        pe_order = []
        for p_ in range(RC):
            for k_ in range(4):
                pe_order.append((("tr", p_, k_), {1: 2, 3: 3 + 5}.get(k_, 0)))
            for lv_ in range(1, 6):
                pe_order.append((("H", p_, lv_), 6))
            pe_order += [(("w1", p_), 0), (("akv", p_), 2), (("w2", p_), 3)]
            pe_order += [(("y", p_, c_), 1) for c_ in range(NCH)]
        PREP = 12
        issued, filled = {}, PREP * DC
        for key, n_ in pe_order:
            issued[key] = min(filled, NF * DC)
            filled += n_
        assert filled - 6 >= NF * DC, filled

        def qchunk(kind, i, part):
            if i < 4:
                return {"sb": 0, "fox": 4}[kind] + 2 * part + i // 2, 64 * (i % 2)
            return 8 + part, {"sb": 0, "fox": 64}[kind]


        block = ctx.enter_context(nc.Block())

        def follow(eng, chain):
            count = {}

            def done(ins, s=chain):
                count[s] = count.get(s, 0) + 1
                ins.then_inc(sem(s), 1)
                eng.wait_ge(sem(s), count[s])
            return done

        @block.sync
        def _(sp):
            for t in range(NT):
                sp.dma_start(h[:, t, :], x[t * P:(t + 1) * P, :]).then_inc(sem("x_in"), 16)
            sp.dma_start(metax[0:META, :], meta).then_inc(sem("x_in"), 16)
            par = sem("params_in")
            for dst, src in ((g1c, g1.rearrange("(c p) -> p c", p=P)), (muc, mu.rearrange("(c p) -> p c", p=P)),
                             (w0c, w0.rearrange("(c p) -> p c", p=P)), (a0c, a0.rearrange("(c p) -> p c", p=P)),
                             (kkc, k_k.rearrange("(c h) d -> (h d) c", h=2)),
                             (kac, k_a.rearrange("(c h) d -> (h d) c", h=2)),
                             (rkc, r_k.rearrange("(c h) d -> (h d) c", h=2)),
                             (lgc, ln_g.rearrange("(c p) -> p c", p=P)), (lbc, ln_b.rearrange("(c p) -> p c", p=P)),
                             (qgc[0:64], q_g.rearrange("(p a) -> p a", a=1)), (qgc[64:128], q_g.rearrange("(p a) -> p a", a=1)),
                             (kgc[0:64], k_g.rearrange("(p a) -> p a", a=1)), (kgc[64:128], k_g.rearrange("(p a) -> p a", a=1)),
                             (up_w[0:64, :], w_up), (up_w[64:128, :], a_up),
                             (fb[:], f_b.rearrange("(a n) -> a n", a=1).broadcast_to([P, FH])),
                             (rbias[:, 0:NG], bg.rearrange("(a n) -> a n", a=1).broadcast_to([P, NG])),
                             (rbias[:, NG:], be.rearrange("(a n) -> a n", a=1).broadcast_to([P, NE])),
                             (rw[:, :, 0:NG], wg.rearrange("(c p) n -> p c n", p=P)),
                             (rw[:, :, NG:], we.rearrange("(c p) n -> p c n", p=P))):
                sp.dma_start(dst, src).then_inc(par, 16)
            for i, (_, cols) in enumerate(pieces):
                if RING <= i < N_RING:
                    sp.wait_ge(sem("piece_used"), i - RING + 1)
                if i == N_RING:
                    sp.wait_ge(sem("bonus_moved"), 1)
                if i >= N_RING + 2:
                    sp.wait_ge(sem("fill_psum"), 1 + max(f for f in range(NF) if groups[f][0] == i - 2))
                col = 0
                for c0, n in cols:
                    sp.dma_start(slot(i)[:, :, col:col + n], wv[:, :, c0:c0 + n]).then_inc(slot_sem(i), 16)
                    col += n
            for t in range(NOV):
                sp.dma_start(y_dram[(NE + t) * P:(NE + t + 1) * P, :], h[:, 0, :]).then_inc(sem("y_defined"), 16)
            sp.wait_ge(sem("y_defined"), 16 * NOV)

            def gate_weights(n):
                if n >= 4:
                    sp.wait_ge(sem("gate_psum"), n - 3)
                c0 = C_G + (n % 3) * D + (n // 3) * P
                sp.dma_start(gate_w[:, (n + 1) % 4, :, :], wv[:, :, c0:c0 + P]).then_inc(sem(f"gate_w{n % 4}"), 16)
            sp.wait_ge(sem("fill_psum"), NF)
            sp.wait_ge(sem("w1_psum"), RC)
            for n in range(EARLY_GATES):
                gate_weights(n)
            sp.wait_ge(sem("dve_phase"), 2)
            sp.wait_ge(sem("act_phase"), 2)
            sp.wait_ge(sem("pe_phase"), 2)
            for n in range(EARLY_GATES, 4):
                gate_weights(n)
            sp.wait_ge(sem("fcum_ready"), 2)
            sp.wait_ge(sem("frow_ones"), 1)
            for hh in range(FH):
                sp.dma_start(FL[0:1, hh, :], fcum[hh:hh + 1, :]).then_inc(sem("frows"), 16)
                sp.dma_start(FR[1:2, hh, :], fcum[64 + hh:65 + hh, :]).then_inc(sem("frows"), 16)
            for n in range(4, 3 * DC):
                gate_weights(n)
            sp.wait_ge(sem("dve_phase"), 4)
            sp.wait_ge(sem("act_phase"), 4)
            sp.wait_ge(sem("pe_phase"), 4)
            for dc in range(DC):
                if dc >= 2:
                    sp.wait_ge(sem("proj_psum"), 3 * (dc - 1))
                s = sem(f"proj_w{dc % 2}")
                cs = slice(dc * P, dc * P + P)
                sp.dma_start(wpr[:, dc % 2, 0:3, :], wp_r[:, cs].rearrange("(c p) n -> p c n", p=P)).then_inc(s, 16)
                for b, w in ((1, wp_s), (2, wp_f)):
                    sp.dma_start(wpr[:, dc % 2, 3 * b:3 * b + 2, :], w[0:256, cs].rearrange("(c p) n -> p c n", p=P)).then_inc(s, 16)
                    lo = 64 * (b - 1)
                    sp.dma_start(wpr[lo:lo + 64, dc % 2, 3 * b + 2, :], w[256:320, cs]).then_inc(s, 16)
                if dc == 1:
                    sp.dma_start(wout[:], w_out.rearrange("(c p) n -> p c n", p=P)).then_inc(sem("wout_in"), 16)
            sp.wait_ge(sem("merged_ready"), DC)
            sp.dma_start(g2b[:], g2.rearrange("(a n) -> a n", a=1).broadcast_to([P, D])).then_inc(sem("g2_in"), 16)
            sp.wait_ge(sem("pe_phase"), 5)
            sp.wait_ge(sem("dve_phase"), 5)
            sp.wait_ge(sem("act_phase"), 5)
            for t in range(NE):
                if t == 2:
                    for i in range(NT):
                        sp.wait_ge(sem("n2_ready"), i + 1)
                        sp.dma_start(n2_dram[i * P:(i + 1) * P, :], n2[:, i, :]).then_inc(sem("n2_out"), 16)
                if t >= 2:
                    sp.wait_ge(sem("gu_psum"), t - 1)
                s = t % 2
                sp.dma_start(w1[:, s, :, 0:DE], m_gate[t, :, :].rearrange("(c p) n -> p c n", p=P)).then_inc(sem(f"moe_w{s}"), 16)
                sp.dma_start(w1[:, s, :, DE:], m_up[t, :, :].rearrange("(c p) n -> p c n", p=P)).then_inc(sem(f"moe_w{s}"), 16)
                if t >= 2:
                    sp.wait_ge(sem("down_psum"), t - 1)
                sp.dma_start(w2[:, s, :, :], m_down[t, :, :].rearrange("(c p) n -> p c n", p=P)).then_inc(sem(f"moe_d{s}"), 16)
                if t >= 2:
                    sp.wait_ge(sem("y_low"), t - 1)
                    sp.wait_ge(sem("y_high"), t - 1)
                    sp.dma_start(y_dram[(t - 2) * P:(t - 1) * P, :], yo[:, t % 2, :]).then_inc(sem(f"y_out{t % 2}"), 16)
            for t in range(NE - 2, NE):
                sp.wait_ge(sem("y_low"), t + 1)
                sp.wait_ge(sem("y_high"), t + 1)
                sp.dma_start(y_dram[t * P:(t + 1) * P, :], yo[:, t % 2, :]).then_inc(sem(f"y_out{t % 2}"), 16)
            sp.wait_ge(sem("ov_ready"), 1)
            sp.wait_ge(sem("y_defined"), 16 * NOV)
            n_ov = sp.value_load(ovi[0:1, 0:1], min_val=0, max_val=NOV)
            with sp.Fori(0, NOV) as k:
                with sp.If(k < n_ov):
                    e = sp.value_load(ovi[0:1, bass.ds(k + 1, 1)], min_val=0, max_val=NE - 1)
                    sp.wait_ge(sem("down_psum"), k + NE)
                    for dst, src, ready in ((w1[:, 0, :, 0:DE], m_gate, sem("moe_w0")), (w1[:, 0, :, DE:], m_up, sem("moe_w0")),
                                            (w2[:, 0, :, :], m_down, sem("moe_d0"))):
                        sp.dma_start(dst, src[bass.ds(e, 1), :, :].rearrange("e (c p) n -> p (e c) n", p=P)).then_inc(ready, 16)
                    sp.wait_ge(sem("y_low"), k + NE + 1)
                    sp.wait_ge(sem("y_high"), k + NE + 1)
                    sp.dma_start(y_dram.rearrange("(t p) n -> t p n", p=P)[bass.ds(k + NE, 1), :, :].rearrange("t p n -> p (t n)"),
                                 yo[:, 0, :]).then_inc(sem("y_out0"), 16)
            sp.wait_ge(sem("y_out0"), n_ov * 16 + NE * 8)
            sp.wait_ge(sem("y_out1"), NE * 8)
            sp.sem_inc(sem("y_stored"), 1)
            for t in range(NT):
                sp.wait_ge(sem("out_ready"), t + 1)
                sp.dma_start(out[t * P:(t + 1) * P, :], h[:, t, :]).then_inc(sem("out_out"), 16)
            sp.wait_ge(sem("out_out"), 16 * NT)
            sp.wait_ge(sem("n2_out"), 16 * NT)

        @block.gpsimd
        def _(pool):
            done = follow(pool, "pool_chain")
            g = nc.gpsimd

            def masked(ap, fill_in, op, pattern, base_, mult, fill=0.0):
                done(g.memset(ap, fill_in))
                done(g.affine_select(out=ap, in_=ap, pattern=pattern, compare_op=op, fill=fill, base=base_,
                                     channel_multiplier=mult))

            done(g.memset(ident[:], 1.0))
            done(g.affine_select(out=ident[:], in_=ident[:], pattern=[[1, P]], compare_op=ALU.is_equal, fill=0.0, base=0,
                                 channel_multiplier=-1), "ident_ready")
            done(g.memset(ones[:], 1.0))
            done(g.memset(neg_ones[:], -1.0))
            masked(tri_le[:], 1.0, ALU.is_ge, [[1, P]], 0, -1)
            masked(tri_lt[:], 1.0, ALU.is_gt, [[1, P]], 0, -1)
            masked(tri_sb[:], -1.0, ALU.is_ge, [[-1, P]], 0, 1)
            masked(neg_sb[:], 0.0, ALU.is_gt, [[1, P]], 0, -1, NEG)
            masked(neg_fox[:], 0.0, ALU.is_ge, [[-1, P]], 0, 1, NEG)
            done(g.memset(head_ones[:], 0.0))
            for i in range(2):
                done(g.memset(head_ones[64 * i:64 * i + 64, 64 * i:64 * i + 64], 1.0))
            for i in range(2):
                q = slice(64 * i, 64 * i + 64)
                masked(ident2[q, :], 1.0, ALU.is_equal, [[1, CH]], 0, -1)
                masked(strict_st[q, :], 1.0, ALU.is_gt, [[1, CH]], 0, -1)
                masked(strict_ts[q, :], 1.0, ALU.is_gt, [[-1, CH]], 0, 1)
                masked(incl_st[q, :], 1.0, ALU.is_ge, [[1, CH]], 0, -1)
            for lv in range(6):
                m = 1 << lv
                nb = CH // (2 * m)
                for i in range(2):
                    q = slice(64 * i, 64 * i + 64)
                    a = mask_tmp[q, lv, :].rearrange("p (b w) -> p b w", b=nb)
                    done(g.memset(a, 1.0))
                    done(g.affine_select(out=a, in_=a, pattern=[[-2 * m, nb], [0, 2 * m]], compare_op=ALU.is_ge, fill=0.0, base=-m, channel_multiplier=1))
                    done(g.affine_select(out=a, in_=a, pattern=[[2 * m, nb], [0, 2 * m]], compare_op=ALU.is_gt, fill=0.0, base=2 * m, channel_multiplier=-1))
                    done(g.affine_select(out=a, in_=a, pattern=[[0, nb], [-1, 2 * m]], compare_op=ALU.is_gt, fill=0.0, base=m, channel_multiplier=0))
                    done(g.tensor_copy(lev_ts[q, lv, :], mask_tmp[q, lv, :]))
                    done(g.memset(a, 1.0))
                    done(g.affine_select(out=a, in_=a, pattern=[[2 * m, nb], [0, 2 * m]], compare_op=ALU.is_gt, fill=0.0, base=m, channel_multiplier=-1))
                    done(g.affine_select(out=a, in_=a, pattern=[[-2 * m, nb], [0, 2 * m]], compare_op=ALU.is_ge, fill=0.0, base=0, channel_multiplier=1))
                    done(g.affine_select(out=a, in_=a, pattern=[[0, nb], [1, 2 * m]], compare_op=ALU.is_ge, fill=0.0, base=-m, channel_multiplier=0))
                    done(g.tensor_copy(lev_st[q, lv, :], mask_tmp[q, lv, :]))
            done(g.memset(reset[:], 1.0))
            done(g.memset(reset[:, 0:L:CH], 0.0))
            done(g.iota(iota_f[:], [[1, P]], base=0, channel_multiplier=0, allow_small_or_imprecise_dtypes=True))
            done(g.iota(iota_row[:], [[1, NE]], base=0, channel_multiplier=0, allow_small_or_imprecise_dtypes=True))
            done(g.iota(tokid[:], [[P, NT]], base=0, channel_multiplier=1, allow_small_or_imprecise_dtypes=True), "consts_ready")
            pool.wait_ge(sem("n2_out"), 16 * NT)
            for t in range(NE):
                pool.wait_ge(sem("idx_ready"), t + 1)
                if t >= 2:
                    pool.wait_ge(sem("xgT_psum"), 2 * t - 2)
                g.indirect_dma_start(out=xg[:, t % 2, :], out_offset=None, in_=n2_dram[:, :],
                                     in_offset=bass.IndirectOffsetOnAxis(ap=idx[:, t % 2:t % 2 + 1], axis=0)).then_inc(sem(f"xg_in{t % 2}"), 16)
            pool.wait_ge(sem("ov_ready"), 1)
            n_ov = pool.value_load(ovi[0:1, 0:1], min_val=0, max_val=NOV)
            with pool.Fori(0, NOV) as k:
                with pool.If(k < n_ov):
                    pool.wait_ge(sem("idx_ready"), k + NE + 1)
                    pool.sem_inc(sem("pool_go"), 1)
                    g.indirect_dma_start(out=xg[:, 0, :], out_offset=None, in_=n2_dram[:, :],
                                         in_offset=bass.IndirectOffsetOnAxis(ap=idx[:, 0:1], axis=0)).then_inc(sem("xg_in0"), 16)
            pool.wait_ge(sem("y_stored"), 1)
            for t in range(NT):
                for j in range(2):
                    if t >= 1:
                        pool.wait_ge(sem("ysel_used"), 2 * (t - 1) + j + 1)
                    g.indirect_dma_start(out=ysel[:, j, :], out_offset=None, in_=y_dram[:, :],
                                         in_offset=bass.IndirectOffsetOnAxis(ap=rows[:, 2 * t + j:2 * t + j + 1], axis=0)).then_inc(sem(f"ysel_in{j}"), 16)

        @block.scalar
        def _(act):
            a = nc.scalar
            done = follow(act, "act_chain")

            def inverse_root(z, s, scale=1.0):
                a.preload_act_table_set("natural_log")
                done(a.activation(z, z, ACT.Ln, scale=scale))
                done(a.activation(z, z, ACT.Exp, scale=-0.5), s)
            act.wait_ge(sem("x_in"), 16 * (NT + 1))
            for t in range(NT):
                done(a.activation(xs[:, t, :], h[:, t, :], ACT.Square, accum_out=stat[:, t:t + 1]), "ss_ready")
            done(a.activation(tmp_shift[0:META, :, :].rearrange("p a b -> p (a b)")[:, 0:D], metax[0:META, :], ACT.Square,
                              accum_out=stat[0:META, 4:5]), "ss_ready")
            act.wait_ge(sem("ms_ready"), 2)
            inverse_root(stat[:, 0:4], "rstd_ready")
            inverse_root(stat[0:META, 4:5], "rstd_ready")
            act.wait_ge(sem("params_in"), 320)
            done(a.mul(qg8, qgc, 0.125), "qg8_ready")
            for c in range(DC):
                act.wait_ge(sem("xT_psum"), c + 1)
                done(a.activation(nT[:, c, META:L], ps[:, c % 4, :], ACT.Copy, scale=g1c[:, c:c + 1]), "nT_ready")
            n = 0
            for j in range(SC):
                act.wait_ge(sem("chunk_psum"), n + 1)
                done(a.activation(U[:, j, 1:L + 1].rearrange("p (a b) -> p a b", a=2), ps[:, 2 * (n % 2):2 * (n % 2) + 2, 0:HALF], ACT.Copy), "chunk_out")
                n += 1
            done(a.activation(stat[:, 8:9], stat[:, 0:1], ACT.Copy), "act_phase")

            out_n = [0]

            def group_out():
                f = out_n[0]
                out_n[0] += 1
                _, kind, j, i = groups[f]
                act.wait_ge(sem("fill_psum"), f + 1)
                b = 2 + f % 2
                if kind == "q":
                    dst = QK[:, j, i * HALF:(i + 1) * HALF]
                    if j != 8:
                        done(a.activation(dst, ps[:, b, 0:HALF], ACT.Copy, scale=0.125 if j < 2 else 1.0), "fill_out")
                    else:
                        done(a.activation(dst[0:64], ps[0:64, b, 0:HALF], ACT.Copy, scale=0.125))
                        done(a.activation(dst[64:128], ps[64:128, b, 0:HALF], ACT.Copy), "fill_out")
                else:
                    r = KT[i][1]
                    if j == 0:
                        done(a.activation(V[0:r, i, 0:SW], ps[0:r, b, 0:SW], ACT.Copy), "fill_out")
                    else:
                        done(a.activation(V[0:r, i, SW:], ps[0:r, b, 0:SW], ACT.Copy))
                        done(a.activation(flog[0:r, i, :], ps[0:r, b, SW:SW + FH], ACT.Copy), "fill_out")

            def groups_out(key):
                while out_n[0] < NF and DC * (out_n[0] + 1) <= issued[key]:
                    group_out()

            act.wait_ge(sem("dve_phase"), 1)
            done(a.activation(U[0:64, 9, 1:], U[0:64, 9, 1:], ACT.Tanh), "wd_ready")
            for c in range(RC):
                act.wait_ge(sem("wa_psum"), 2 * c + 1)
                pin = psf[:, 0:1024].rearrange("p (a b) -> p a b", a=2)[:, :, 0:HALF]
                done(a.activation(ta[:, c, :].rearrange("p (a b) -> p a b", a=2), pin, ACT.Sigmoid, bias=w0c[:, c:c + 1]), "wa_used")
                act.wait_ge(sem("wa_psum"), 2 * c + 2)
                pin = psf[:, 3072:4096].rearrange("p (a b) -> p a b", a=2)[:, :, 0:HALF]
                done(a.activation(tb[:, c, :].rearrange("p (a b) -> p a b", a=2), pin, ACT.Sigmoid, bias=a0c[:, c:c + 1]), "wa_used")
            for _ in range(2):
                group_out()
            for c in range(RC):
                act.wait_ge(sem("kk_used"), c + 1)
                inverse_root(Kt[:, c, 0:L], "kk_rs", float(2 ** 30))
            for _ in range(4):
                group_out()
            act.wait_ge(sem("cum_ready"), RC)
            for c in range(RC):
                pv = Pc[:, c, :].rearrange("p (n t) -> p n t", t=CH + 1)
                done(a.activation(pv[:, 0:NCH - 1, 1:], tc_[:, c, 0:(NCH - 1) * CH].rearrange("p (n t) -> p n t", t=CH), ACT.Exp, scale=-DECAY))
                done(a.activation(pv[:, NCH - 1, 1:1 + L % CH], tc_[:, c, (NCH - 1) * CH:L], ACT.Exp, scale=-DECAY))
                done(a.activation(tc_[:, c, :], tc_[:, c, :], ACT.Exp, scale=DECAY), "decay_ready")
            while out_n[0] < PREP:
                group_out()
            for p in range(RC):
                for q, dst in enumerate((AtT, BtT, KtT, VT)):
                    act.wait_ge(sem("tr_psum"), 4 * p + q + 1)
                    done(a.activation(dst.rearrange("p n t -> p (n t)"), psf[:, 3072 * (q % 2):3072 * (q % 2) + LP], ACT.Copy), "tr_used")
                    groups_out(("tr", p, q))
                for lv in range(1, 6):
                    act.wait_ge(sem("H_psum"), 5 * p + lv)
                    done(a.activation(Hm.rearrange("p n t -> p (n t)"), psf[:, 2048:2048 + LP], ACT.Copy), "H_ready")
                    groups_out(("H", p, lv))
                act.wait_ge(sem("w1_psum"), p + 1)
                done(a.activation(W1T.rearrange("p n t -> p (n t)"), psf[:, 0:LP], ACT.Copy), "w1_ready")
                act.wait_ge(sem("akv_psum"), p + 1)
                done(a.activation(Hm.rearrange("p n t -> p (n t)"), psf[:, 3072:3072 + LP], ACT.Copy), "akv_ready")
                act.wait_ge(sem("w2_psum"), p + 1)
                done(a.activation(W2.rearrange("p n t -> p (n t)"), psf[:, 2048:2048 + LP], ACT.Copy), "w2_ready")
                groups_out(("w2", p))
                for c in range(NCH):
                    act.wait_ge(sem("y_psum"), NCH * p + c + 1)
                    w = min(CH, L - c * CH)
                    o = max(0, META - c * CH)
                    done(a.activation(yT[0][:, p, c * CH + o - META:c * CH + w - META], ps[:, 5 + 2 * (c % 2), o:w], ACT.Copy), "y_out_rwkv")
                    groups_out(("y", p, c))
                    if p == RC - 1:
                        if c < 6:
                            if c >= 1:
                                act.wait_ge(sem("norm_psum"), c)
                            done(a.activation(tmp_shift[:, 0, :], QK[:, 4 + c, :], ACT.Square), "fsq_ready")
                        if 1 <= c <= 6:
                            act.wait_ge(sem("fms_ready"), c)
                            inverse_root(tmp_shift[slice(0, P) if c <= 4 else slice(64, P), 1, :], "frs_ready")
            done(a.activation(Rt[:, :, 0:SEQ], yT[0][:], ACT.Square), "act_phase")
            for c in range(RC):
                act.wait_ge(sem("var_ready"), c + 1)
                inverse_root(Kt[:, c, 0:SEQ], "ln_rs")

            act.wait_ge(sem("f_pre"), 1)
            fl = flog.rearrange("p a b -> p (a b)")
            done(a.activation(fl[:, 0:20], fl[:, 0:20], ACT.Exp, scale=-1.0))
            done(a.activation(fl[0:16, 20:25], fl[0:16, 20:25], ACT.Exp, scale=-1.0))
            done(a.activation(fl[:, 0:20], fl[:, 0:20], ACT.Ln, bias=1.0))
            done(a.activation(fl[0:16, 20:25], fl[0:16, 20:25], ACT.Ln, bias=1.0), "f_ready")
            act.wait_ge(sem("dve_phase"), 2)
            act.wait_ge(sem("pe_phase"), 2)
            act.wait_ge(sem("fcum_psum"), 1)
            pin = psf[:, 0:1024].rearrange("p (a b) -> p a b", a=2)[0:FH, :, 0:HALF]
            done(a.activation(fcum[0:FH, :].rearrange("p (a b) -> p a b", a=2), pin, ACT.Copy, scale=-1.0), "fcum_ready")
            done(a.activation(fcum[64:64 + FH, :].rearrange("p (a b) -> p a b", a=2), pin, ACT.Copy), "fcum_ready")
            a.preload_act_table_set("natural_log_exp_and_others")
            u = 0
            for hh in range(SH):
                for i, (k0, r) in enumerate(KT):
                    n = min(SEQ, L - k0)
                    act.wait_ge(sem("z_psum"), u + 1)
                    if hh >= 1:
                        act.wait_ge(sem("sb_used"), hh)
                    if u >= 2:
                        act.wait_ge(sem("sp_ready"), u - 1)
                    e = s_a[0:r, u % 2, 0:n]
                    z = ps[0:r, i, 0:n]
                    done(a.activation(e, z, ACT.Abs))
                    done(a.activation(e, e, ACT.Exp, scale=-1.0))
                    done(a.activation(e, e, ACT.Ln, bias=1.0), "l_ready")
                    u += 1
                for i, (k0, r) in enumerate(KT):
                    n = min(SEQ, L - k0)
                    act.wait_ge(sem("w_psum"), 5 * hh + i + 1)
                    done(a.activation(s_c[i][0:r, 0:n], ps[0:r, i, 0:n], ACT.Exp), "A_ready")
            done(a.activation(stat[:, 8:9], stat[:, 0:1], ACT.Copy), "act_phase")

            act.wait_ge(sem("dve_phase"), 3)
            u = 0
            for hh in range(FH):
                for i in range(NT):
                    kn = META + P * (i + 1)
                    act.wait_ge(sem("m_ready"), u + 1)
                    if u >= 2:
                        act.wait_ge(sem("pT_psum"), u - 1)
                    done(a.activation(p_f[:, u % 2, 0:kn], psf[:, 1024 * (u % 2):1024 * (u % 2) + kn], ACT.Exp,
                                      bias=stat[:, 9 + u % 2:10 + u % 2], accum_out=stat[:, 11 + u % 2:12 + u % 2]), "p_ready")
                    u += 1
            act.wait_ge(sem("pT_psum"), u)
            done(a.activation(stat[:, 8:9], stat[:, 0:1], ACT.Copy), "act_phase")

            for n in range(3 * DC):
                act.wait_ge(sem("gate_out"), n + 1)
                done(a.activation(gate(n), gate(n), ACT.Sigmoid), "gate_ready")
            done(a.activation(stat[:, 8:9], stat[:, 0:1], ACT.Copy), "act_phase")

            for t in range(NT + 1):
                if t < NT:
                    act.wait_ge(sem("h_ready"), t + 1)
                    done(a.activation(h_sq[:], h[:, t, :], ACT.Square, accum_out=stat[:, t:t + 1]), "ss2_ready")
                    act.wait_ge(sem("ms2_ready"), t + 1)
                    inverse_root(stat[:, t:t + 1], "rstd2_ready")
                if t >= 1:
                    act.wait_ge(sem("n2T_psum"), t)
                    b = 6 * ((t - 1) % 2)
                    pin = psf[:, 512 * b:512 * b + D].rearrange("p (c n) -> p c n", c=DC)
                    done(a.activation(n2T[:, :, (t - 1) * P:t * P], pin, ACT.Copy), "n2T_ready")

            act.wait_ge(sem("dve_phase"), 5)
            act.wait_ge(sem("lg_ready"), 1)
            done(a.activation(rt[:, 1, 0:NT * NG], rt[:, 1, 0:NT * NG], ACT.Exp))
            done(a.activation(rt[:, 2, 0:NT], rt[:, 2, 0:NT], ACT.Exp), "pe_exp")

            def rows_T(t, s, slot_free):
                for k in range(2):
                    act.wait_ge(sem("xgT_psum"), t * 2 + (k + 1))
                    if slot_free:
                        act.wait_ge(sem("gu_psum"), t - 1)
                    a.activation(xgT[:, s, 4 * k:4 * k + 4, :].rearrange("p c n -> p (c n)"), ps[:, k, :], ACT.Copy).then_inc(sem("xgT_ready"), 1)

            def silu(t, s, bank, slot_free):
                act.wait_ge(sem("gu_psum"), t + 1)
                if slot_free:
                    act.wait_ge(sem("hT_psum"), t - 1)
                a.activation(hg[:, s, 0:DE], ps[:, bank, 0:DE], ACT.Silu).then_inc(sem("silu_ready"), 1)

            def hidden_T(t, s, slot_free):
                act.wait_ge(sem("hT_psum"), t + 1)
                if slot_free:
                    act.wait_ge(sem("down_psum"), t - 1)
                a.activation(hT[:, s, :, :].rearrange("p c n -> p (c n)"), ps[:, 3, 0:2 * P], ACT.Copy).then_inc(sem("hT_ready"), 1)

            def y_low(t, s, stores):
                act.wait_ge(sem("down_psum"), t + 1)
                if stores is not None:
                    act.wait_ge(sem(f"y_out{s}"), stores)
                a.activation(yo[:, s, 0:512], ps[:, 4, :], ACT.Copy).then_inc(sem("y_low"), 1)
            rows_T(0, 0, False)
            for t in range(NE + 1):
                if t < NE:
                    silu(t, t % 2, 2 + 4 * (t % 2), t >= 2)
                if t >= 1:
                    hidden_T(t - 1, (t - 1) % 2, t >= 3)
                if t + 1 < NE:
                    rows_T(t + 1, (t + 1) % 2, t >= 1)
                if t >= 1:
                    y_low(t - 1, (t - 1) % 2, 16 * ((t - 1) // 2) if t >= 3 else None)
            act.wait_ge(sem("ov_ready"), 1)
            n_ov = act.value_load(ovi[0:1, 0:1], min_val=0, max_val=NOV)
            with act.Fori(0, NOV) as k:
                with act.If(k < n_ov):
                    t = k + NE
                    act.wait_ge(sem("y_out0"), k * 16 + NE * 8)
                    rows_T(t, 0, False)
                    silu(t, 0, 2, False)
                    hidden_T(t, 0, False)
                    y_low(t, 0, None)

        @block.vector
        def _(dve):
            v = nc.vector
            done = follow(dve, "dve_chain")
            ts, tt, stt = v.tensor_scalar, v.tensor_tensor, v.scalar_tensor_tensor
            dve.wait_ge(sem("ss_ready"), NT + 1)
            done(ts(stat[:, 0:4], stat[:, 0:4], 1.0 / D, EPS, ALU.mult, ALU.add), "ms_ready")
            done(ts(stat[0:META, 4:5], stat[0:META, 4:5], 1.0 / D, EPS, ALU.mult, ALU.add), "ms_ready")
            dve.wait_ge(sem("rstd_ready"), 2)
            for t in range(NT):
                done(ts(xs[:, t, :], h[:, t, :], stat[:, t:t + 1], None, ALU.mult), "xs_ready")
            done(ts(metax[0:META, :], metax[0:META, :], stat[0:META, 4:5], None, ALU.mult), "xs_ready")
            dve.wait_ge(sem("params_in"), 320)
            dve.wait_ge(sem("xT_psum"), DC + 1)
            done(tt(nT[:, :, 0:META], ps[:, 4, 0:DC * META].rearrange("p (c n) -> p c n", c=DC),
                    g1c.rearrange("p (c a) -> p c a", a=1).broadcast_to([P, DC, META]), ALU.mult), "nT_meta")
            for j in range(SC):
                done(v.memset(U[:, j, 0:1], 0.0))
            for j in range(SC):
                dve.wait_ge(sem("chunk_out"), j + 1)
                d_ = tmp_shift[:, 1, :]
                done(tt(d_, U[:, j, 0:L], U[:, j, 1:L + 1], ALU.subtract))
                done(stt(U[:, j, 1:L + 1], d_, muc[:, j:j + 1], U[:, j, 1:L + 1], ALU.mult, ALU.add))
            done(v.memset(stat[:, 13:14], 0.0), "dve_phase")

            dve.wait_ge(sem("act_phase"), 1)
            r_, k_, v_ = U[:, 0:3, 1:], U[:, 3:6, 1:], U[:, 6:9, 1:]
            for t_ in (At, Rt, Bt, Kt):
                done(v.memset(t_[:, :, L:LP], 0.0))
            done(v.memset(Pc[:], 1.0))
            dve.wait_ge(sem("consts_ready"), 1)
            for c in range(RC):
                dve.wait_ge(sem("wa_used"), 2 * c + 1)
                done(v.tensor_tensor_scan(tc_[:, c, :], reset[:], ta[:, c, :], 0.0, ALU.mult, ALU.add), "cum_ready")
            for c in range(RC):
                done(ts(At[:, c, 0:L], k_[:, c, :], kkc[:, c:c + 1], None, ALU.mult))
                done(tt(Bt[:, c, 0:L], At[:, c, 0:L], At[:, c, 0:L], ALU.mult), "kk_sq")
            for c in range(RC):
                dve.wait_ge(sem("kk_psum"), c + 1)
                d_ = Kt[:, c, 0:L].rearrange("p (a b) -> p a b", a=2)
                done(ts(d_, psf[:, 2048:3072].rearrange("p (a b) -> p a b", a=2)[:, :, 0:HALF], 1e-24, None, ALU.max), "kk_used")
            AL, RL, BL, KL = (z[:, :, 0:L] for z in (At, Rt, Bt, Kt))
            dve.wait_ge(sem("kk_rs"), RC)
            done(stt(AL, AL, 32768.0, KL, ALU.mult, ALU.mult))
            dve.wait_ge(sem("wa_used"), 2 * RC)
            done(tt(BL, AL, tb[:], ALU.mult))
            for c in range(RC):
                done(ts(tb[:, c, :], tb[:, c, :], 1.0, kac[:, c:c + 1], ALU.subtract, ALU.mult))
                done(stt(KL[:, c, :], tb[:, c, :], 1.0, k_[:, c, :], ALU.add, ALU.mult))
                done(stt(tb[:, c, :], r_[:, c, :], rkc[:, c:c + 1], KL[:, c, :], ALU.mult, ALU.mult), "rk_ready")
            dve.wait_ge(sem("decay_ready"), RC)
            for c in range(RC):
                pv = Pc[:, c, :].rearrange("p (n t) -> p n t", t=CH + 1)
                for dst, src, o, sgn in ((At, At, 0, -1.0), (Rt, None, 1, 1.0)):
                    for n0, n1, w in ((0, NCH - 1, CH), (NCH - 1, NCH, L % CH)):
                        lo = n0 * CH
                        hi = lo + (n1 - n0) * w
                        so = dst[:, c, lo:hi].rearrange("p (n t) -> p n t", t=w)
                        si = so if src is not None else r_[:, c, lo:hi].rearrange("p (n t) -> p n t", t=w)
                        done(stt(so, si, sgn, pv[:, n0:n1, o:o + w], ALU.mult, ALU.mult))
            done(tt(BL, BL, tc_[:], ALU.mult))
            done(tt(KL, KL, tc_[:], ALU.mult), "tilde_ready")
            for c in range(RC):
                dve.wait_ge(sem("bonus_psum"), c + 1)
                done(tt(tb[:, c, :].rearrange("p (a b) -> p a b", a=2), psf[:, 2048:3072].rearrange("p (a b) -> p a b", a=2)[:, :, 0:HALF],
                        v_[:, c, :].rearrange("p (a b) -> p a b", a=2), ALU.mult), "bonus_used")
            done(v.tensor_copy(tc_[:], tb[:]), "bonus_moved")
            dve.wait_ge(sem("qg8_ready"), 1)
            bc = lambda m_: m_.rearrange("p (a t) -> p a t", a=1).broadcast_to([P, NCH, CH])
            for p in range(RC):
                for q, (dst, msk) in enumerate(((AKT, strict_st), (RKT, incl_st), (NTm, strict_st), (RBT, incl_st), (Nm, strict_ts))):
                    dve.wait_ge(sem("g_psum"), 5 * p + q + 1)
                    done(tt(dst[:], psf[:, 1024 * (2 + q % 2):1024 * (2 + q % 2) + LP].rearrange("p (n t) -> p n t", t=CH), bc(msk[:]), ALU.mult), "g_used")
                done(v.tensor_copy(Tm[:], bc(ident2[:])))
                done(v.copy_predicated(Tm[:], bc(lev_ts[:, 0, :]), Nm[:]))
                done(v.tensor_copy(TTm[:], bc(ident2[:])))
                done(v.copy_predicated(TTm[:], bc(lev_st[:, 0, :]), NTm[:]), "T_ready")
                for lv in range(1, 6):
                    if lv < 5:
                        dve.wait_ge(sem("G_psum"), 9 * p + 2 * lv - 1)
                        done(v.copy_predicated(Tm[:], bc(lev_ts[:, lv, :]), psf[:, 3072:3072 + LP].rearrange("p (n t) -> p n t", t=CH)))
                    dve.wait_ge(sem("G_psum"), 9 * p + min(2 * lv, 9))
                    done(v.copy_predicated(TTm[:], bc(lev_st[:, lv, :]), psf[:, 0:LP].rearrange("p (n t) -> p n t", t=CH)), "T_ready")
                done(v.memset(Ssb[:], 0.0), "S_ready")
                for c in range(NCH):
                    dve.wait_ge(sem("u_psum"), NCH * p + c + 1)
                    if c == 0:
                        dve.wait_ge(sem("w2_ready"), p + 1)
                    done(tt(Usb[:], ps[:, 6, 0:CH], W2[:, c, :], ALU.add), "U_ready")
                    if c < NCH - 1:
                        dve.wait_ge(sem("s_psum"), (NCH - 1) * p + c + 1)
                        done(tt(Ssb[:], ps[:, 6, 128:128 + CH], Ssb[:], ALU.add))
                        done(ts(Ssb[:], Ssb[:], Pc[:, p, c * (CH + 1) + CH:(c + 1) * (CH + 1)], None, ALU.mult), "S_ready")
                    if p == RC - 1:
                        if 2 <= c <= 7:
                            m = c - 2
                            q = slice(0, P) if m < 4 else slice(64, P)
                            gain = (qg8, qg8, kgc, kgc, qg8, kgc)[m]
                            dve.wait_ge(sem("frs_ready"), c - 1)
                            done(stt(QK[q, 4 + m, :], QK[q, 4 + m, :], gain[q], tmp_shift[q, 1, :], ALU.mult, ALU.mult))
                        if 1 <= c <= 6:
                            q = slice(0, P) if c <= 4 else slice(64, P)
                            dve.wait_ge(sem("norm_psum"), c)
                            done(ts(tmp_shift[q, 1, :].rearrange("p (a b) -> p a b", a=2), ps[q, 2:4, 0:HALF], 1.0 / HD, EPS, ALU.mult, ALU.add), "fms_ready")
            dve.wait_ge(sem("fill_out"), NF)
            done(tt(flog[:, 0:4, :], flog[:, 0:4, :], fb[:].rearrange("p (a n) -> p a n", a=1).broadcast_to([P, 4, FH]), ALU.add))
            done(tt(flog[0:16, 4, :], flog[0:16, 4, :], fb[0:16, :], ALU.add), "f_pre")

            def gate_logits(n):
                dve.wait_ge(sem("gate_psum"), n + 1)
                done(v.tensor_copy(gate(n), ps[:, 5 + 2 * (n % 2), :]), "gate_out")

            dve.wait_ge(sem("act_phase"), 2)
            for c in range(RC + 1):
                if c < RC:
                    dve.wait_ge(sem("ln_psum"), 2 * c + 2)
                    mean, var, sq, y_ = (z[:, c, 0:SEQ] for z in (Bt, Kt, At, yT[0]))
                    done(ts(mean, ps[:, 0, :], 1.0 / HD, None, ALU.mult))
                    done(tt(sq, mean, mean, ALU.mult))
                    done(stt(var, ps[:, 1, :], 1.0 / HD, sq, ALU.mult, ALU.subtract), "ln_used")
                    done(ts(var, var, 0.0, LN_EPS, ALU.max, ALU.add), "var_ready")
                    done(tt(y_, y_, mean, ALU.subtract))
                if c >= 1:
                    var, y_ = Kt[:, c - 1, 0:SEQ], yT[0][:, c - 1, :]
                    dve.wait_ge(sem("ln_rs"), c)
                    done(tt(y_, y_, var, ALU.mult))
                    done(ts(y_, y_, lgc[:, c - 1:c], lbc[:, c - 1:c], ALU.mult, ALU.add))
                    done(tt(y_, y_, tc_[:, c - 1, META:], ALU.add))
                    if c < RC:
                        gate_logits(c - 1)
            done(v.memset(stat[:, 13:14], 0.0), "dve_phase")
            for n in range(RC - 1, EARLY_GATES):
                gate_logits(n)

            dve.wait_ge(sem("pe_phase"), 2)
            done(v.memset(FL[0:2, :, :], 1.0))
            done(v.memset(FR[0:2, :, :], 1.0), "frow_ones")
            u = 0
            for hh in range(SH):
                for i, (k0, r) in enumerate(KT):
                    n = min(SEQ, L - k0)
                    dve.wait_ge(sem("l_ready"), u + 1)
                    if hh >= 1:
                        dve.wait_ge(sem("w_psum"), 5 * hh)
                    done(stt(s_b[i][0:r, 0:n], ps[0:r, i, 0:n], 0.0, s_a[0:r, u % 2, 0:n], ALU.max, ALU.add))
                    q0 = META if i == 0 else 0
                    w = r - q0
                    done(tt(s_b[i][0:r, 0:w], s_b[i][0:r, 0:w], tri_lt[0:r, q0:q0 + w], ALU.mult), "sp_ready")
                    u += 1
                for n in range(EARLY_GATES + max(0, 2 * hh - 1), EARLY_GATES + 2 * hh + 1):
                    gate_logits(n)
                dve.wait_ge(sem("o_psum"), hh + 1)
                row = 64 * (hh % 2) if hh < 4 else 0
                done(v.tensor_copy(yT[1][row:row + 64, hh // 2, :], ps[row:row + 64, 6, :]), "sb_used")
            done(v.memset(stat[:, 13:14], 0.0), "dve_phase")

            dve.wait_ge(sem("act_phase"), 3)
            gates_out = EARLY_GATES + 2 * SH - 1
            u = 0
            for hh in range(FH):
                for i in range(NT):
                    kn = META + P * (i + 1)
                    dve.wait_ge(sem("s_ready"), u + 1)
                    if u >= 2:
                        dve.wait_ge(sem("p_ready"), u - 1)
                    done(v.tensor_reduce(stat[:, 9 + u % 2:10 + u % 2], psf[:, 1024 * (u % 2):1024 * (u % 2) + kn], AX, ALU.max, negate=True), "m_ready")
                    dve.wait_ge(sem("p_ready"), u + 1)
                    done(v.reciprocal(stat[:, 14:15], stat[:, 11 + u % 2:12 + u % 2]))
                    done(ts(p_f[:, u % 2, 0:kn], p_f[:, u % 2, 0:kn], stat[:, 14:15], None, ALU.mult), "pn_ready")
                    dve.wait_ge(sem("pT_psum"), u + 1)
                    if u >= 2:
                        dve.wait_ge(sem("of_psum"), u - 1)
                    nk = i + 1
                    done(v.tensor_copy(pT[:, u % 2, 0:nk, :], ps[:, 4, 0:nk * P].rearrange("p (a b) -> p a b", b=P)))
                    done(v.tensor_copy(pT[0:16, u % 2, nk, :], ps[0:16, 6, 256:256 + P]), "pTs_ready")
                    while gates_out < 3 * DC and 8 * (gates_out + 1) <= 8 * (EARLY_GATES + 2 * SH) + FOX_FILL * 2 * u + FOX_FILL:
                        gate_logits(gates_out)
                        gates_out += 1
                    dve.wait_ge(sem("of_psum"), u + 1)
                    row = 64 * (hh % 2) if hh < 4 else 64
                    done(v.tensor_copy(yT[2][row:row + 64, hh // 2, i * P:(i + 1) * P], ps[row:row + 64, 6, 0:P]), "of_used")
                    u += 1
            done(v.memset(stat[:, 13:14], 0.0), "dve_phase")

            for n in range(gates_out, 3 * DC):
                gate_logits(n)
            dve.wait_ge(sem("pe_phase"), 4)
            n = 0
            for dc in range(DC):
                for b in range(3):
                    dve.wait_ge(sem("gate_ready"), n + 1)
                    dve.wait_ge(sem("proj_psum"), n + 1)
                    dst = merged[:, dc, :] if b == 0 else macc[:]
                    done(tt(dst, gate(n), ps[:, 2 + n % 2, :], ALU.mult), "proj_used")
                    if b > 0:
                        done(tt(merged[:, dc, :], merged[:, dc, :], macc[:], ALU.add), *(["merged_ready"] if b == 2 else []))
                    n += 1
            for t in range(NT):
                for k in range(2):
                    dve.wait_ge(sem("wo_psum"), 2 * t + k + 1)
                    done(tt(h[:, t, 512 * k:512 * k + 512], h[:, t, 512 * k:512 * k + 512], ps[:, 4 + k, :], ALU.add), "wo_used")
                done(v.memset(stat[:, 13:14], 0.0), "h_ready")
                dve.wait_ge(sem("ss2_ready"), t + 1)
                done(ts(stat[:, t:t + 1], stat[:, t:t + 1], 1.0 / D, EPS, ALU.mult, ALU.add), "ms2_ready")
                dve.wait_ge(sem("rstd2_ready"), t + 1)
                if t == 0:
                    dve.wait_ge(sem("g2_in"), 16)
                done(stt(n2[:, t, :], h[:, t, :], stat[:, t:t + 1], g2b[:], ALU.mult, ALU.mult), "n2_ready")
            done(v.memset(stat[:, 13:14], 0.0), "dve_phase")

            NGE = NG + NE
            R = lambda i, w=NE: rt[:, i, 0:NT * w].rearrange("p (t e) -> p t e", t=NT)
            row3 = lambda z, w: z.rearrange("p (t a) -> p t a", a=1).broadcast_to([P, NT, w])
            rep = lambda z, w: z.rearrange("p (a e) -> p a e", a=1).broadcast_to([P, NT, w])
            dve.wait_ge(sem("lg_psum"), 1)
            lg_ps = ps[:, 2, 0:NT * NGE].rearrange("p (t e) -> p t e", t=NT)
            lg, le = R(0, NG), R(3)
            done(tt(lg, lg_ps[:, :, 0:NG], rep(rbias[:, 0:NG], NG), ALU.add))
            done(tt(le, lg_ps[:, :, NG:], rep(rbias[:, NG:], NE), ALU.add))
            gmax = rt[:, 4, 0:NT]

            def first(onehot, vals, mx, w, tmp):
                done(tt(onehot, vals, row3(mx, w), ALU.is_equal))
                done(ts(onehot, onehot, -1000.0, 1000.0, ALU.mult, ALU.add))
                done(tt(onehot, onehot, rep(iota_row[:, 0:w], w), ALU.add))
                done(v.tensor_reduce(tmp, onehot, AX, ALU.min))
                done(tt(onehot, rep(iota_row[:, 0:w], w), row3(tmp, w), ALU.is_equal))

            done(v.tensor_reduce(gmax, lg, AX, ALU.max))
            og = R(5, NG)
            first(og, lg, gmax, NG, rt[:, 6, 0:NT])
            done(tt(R(1, NG), lg, row3(gmax, NG), ALU.subtract))
            done(ts(og, og, 1.0, -NEG, ALU.subtract, ALU.mult))
            le4 = le.rearrange("p t (g e) -> p (t g) e", g=NG)
            done(ts(rt[:, 7, 0:NT * NG], rt[:, 5, 0:NT * NG], -1.0 / -NEG, None, ALU.mult))
            done(tt(le4, le4, rt[:, 5, 0:NT * NG].rearrange("p (t a) -> p t a", a=1).broadcast_to([P, NT * NG, EPG]), ALU.add))
            m1, m2 = rt[:, 8, 0:NT], rt[:, 9, 0:NT]
            oh1, oh2 = R(10), R(11)
            done(v.tensor_reduce(m1, le, AX, ALU.max))
            first(oh1, le, m1, NE, rt[:, 6, 0:NT])
            done(stt(le, oh1, 4 * NEG, le, ALU.mult, ALU.add))
            done(v.tensor_reduce(m2, le, AX, ALU.max))
            first(oh2, le, m2, NE, rt[:, 6, 0:NT])
            done(tt(rt[:, 2, 0:NT], m2, m1, ALU.subtract), "lg_ready")
            done(tt(R(12), oh1, oh2, ALU.add), "assign_ready")
            dve.wait_ge(sem("pe_exp"), 1)
            den, c1, c2 = rt[:, 6, 0:NT], rt[:, 13, 0:NT], rt[:, 13, NT:2 * NT]
            done(v.tensor_reduce(den, R(1, NG), AX, ALU.add))
            done(ts(c1, rt[:, 2, 0:NT], 1.0, None, ALU.add))
            done(tt(c1, c1, den, ALU.mult))
            done(v.reciprocal(c1, c1))
            done(tt(c2, c1, rt[:, 2, 0:NT], ALU.mult))
            dve.wait_ge(sem("rank_psum"), 1)
            rank = R(0)
            done(v.tensor_copy(rank, ps[:, 3, 0:NT * NE].rearrange("p (t e) -> p t e", t=NT)))
            cnt0 = rt[:, 4, NT:NT + NE]
            done(v.tensor_copy(cnt0, ps[:, 3, NT * NE:(NT + 1) * NE]), "counts_out")
            raw = R(7)
            done(v.tensor_copy(raw, rank))
            done(stt(rank, rank, 1.0, R(12), ALU.add, ALU.mult))
            done(ts(rank, rank, -1.0, None, ALU.add))
            def index(t, s, sel):
                v.tensor_tensor(Pm[:], sel, iota_f[:].rearrange("p (a n) -> p a n", a=1).broadcast_to([P, NT, P]),
                                ALU.is_equal).then_inc(sem("pm_ready"), 1)
                dve.wait_ge(sem("idx_psum"), t + 1)
                v.tensor_copy(idx[:, s:s + 1], ps[:, 7, 0:1]).then_inc(sem("idx_ready"), 1)

            def gated(t, s, bank):
                dve.wait_ge(sem("silu_ready"), t + 1)
                v.tensor_tensor(hg[:, s, 0:DE], hg[:, s, 0:DE], ps[:, bank, DE:], ALU.mult).then_inc(sem("hg_ready"), 1)

            def y_high(t, s, stores):
                dve.wait_ge(sem("down_psum"), t + 1)
                if stores is not None:
                    dve.wait_ge(sem(f"y_out{s}"), stores)
                v.tensor_copy(yo[:, s, 512:], ps[:, 5, :]).then_inc(sem("y_high"), 1)

            def tables():
                cnt, ov, inc, exc = (rt[:, 14, i * NE:(i + 1) * NE] for i in range(4))
                done(v.tensor_copy(cnt, cnt0))
                done(ts(ov, cnt, float(P) + 0.5, None, ALU.is_gt))
                for m in (2, 3):
                    done(stt(ov, cnt, m * float(P) + 0.5, ov, ALU.is_gt, ALU.add))
                done(v.tensor_tensor_scan(inc, ones[:, 0:NE], ov, 0.0, ALU.mult, ALU.add))
                done(tt(exc, inc, ov, ALU.subtract))
                base1, base2 = rt[:, 15, 0:NE], rt[:, 15, NE:2 * NE]
                done(ts(base1, iota_row[:], float(P), None, ALU.mult))
                done(ts(base2, exc, float(NE - 1), float(P), ALU.add, ALU.mult))
                done(tt(base2, base2, base1, ALU.subtract))
                over = R(3)
                done(ts(over, raw, float(P) - 0.5, None, ALU.is_gt))
                done(tt(over, over, rep(base2, NE), ALU.mult))
                done(tt(over, over, raw, ALU.add))
                done(tt(over, over, rep(base1, NE), ALU.add))
                for j, oh in enumerate((oh1, oh2)):
                    done(tt(oh, oh, over, ALU.mult))
                    done(v.tensor_reduce(rt[:, 15, 2 * NE + j * NT:2 * NE + (j + 1) * NT], oh, AX, ALU.add))
                    done(v.tensor_copy(rows[:].rearrange("p (t j) -> p j t", j=2)[:, j, :], rt[:, 15, 2 * NE + j * NT:2 * NE + (j + 1) * NT]))
                mk = rt[:, 9, 0:NE]
                done(v.memset(ovf[:], 0.0))
                done(v.tensor_copy(ovf[:, 0:1], inc[:, NE - 1:NE]))
                for k in range(NOV):
                    done(ts(mk, inc, k + 0.5, None, ALU.is_lt))
                    done(v.tensor_reduce(ovf[:, 1 + k:2 + k], mk, AX, ALU.add))
                    done(tt(mk, mk, ov, ALU.mult))
                    done(v.tensor_reduce(ovf[:, 1 + NOV + k:2 + NOV + k], mk, AX, ALU.add))
                    done(ts(ovf[:, 1 + NOV + k:2 + NOV + k], ovf[:, 1 + NOV + k:2 + NOV + k], -float(P), (k + 1) * float(P), ALU.mult, ALU.add))
                done(v.tensor_copy(ovi[:], ovf[:]), "ov_ready")

            def sel_of(e):
                return rank[:, :, e:e + 1].broadcast_to([P, NT, P])
            for t in range(-2, NE + 1):
                if t + 2 < NE:
                    if t >= 0:
                        dve.wait_ge(sem(f"xg_in{t % 2}"), 16 * (t // 2 + 1))
                    if t >= -1:
                        dve.wait_ge(sem("idx_psum"), t + 2)
                    index(t + 2, t % 2, sel_of(t + 2))
                if t == -1:
                    tables()
                if 0 <= t < NE:
                    gated(t, t % 2, 2 + 4 * (t % 2))
                if t >= 1:
                    y_high(t - 1, (t - 1) % 2, 16 * ((t - 1) // 2) if t >= 3 else None)
            n_ov = dve.value_load(ovi[0:1, 0:1], min_val=0, max_val=NOV)
            with dve.Fori(0, NOV) as k:
                with dve.If(k < n_ov):
                    e = dve.value_load(ovi[0:1, bass.ds(k + 1, 1)], min_val=0, max_val=NE - 1)
                    ov_rank = rt[:, 8, 0:NT]
                    dve.wait_ge(sem("down_psum"), k + NE)
                    v.tensor_scalar(ov_rank, rank[:, :, bass.ds(e, 1)].rearrange("p t e -> p (t e)"), ovf[:, bass.ds(k + NOV + 1, 1)], None,
                                    ALU.subtract).then_inc(sem("ov_rank"), 1)
                    dve.wait_ge(sem("ov_rank"), k + 1)
                    index(k + NE, 0, ov_rank.rearrange("p (t a) -> p t a", a=1).broadcast_to([P, NT, P]))
                    gated(k + NE, 0, 2)
                    dve.wait_ge(sem("y_out0"), k * 16 + NE * 8)
                    y_high(k + NE, 0, None)
            for t in range(NT):
                for j, cc in ((0, c1), (1, c2)):
                    dve.wait_ge(sem(f"ysel_in{j}"), 16 * (t + 1))
                    ins = stt(h[:, t, :], ysel[:, j, :], cc[:, t:t + 1], h[:, t, :], ALU.mult, ALU.add)
                    done(ins, "ysel_used")
                done(v.memset(stat[:, 13:14], 0.0), "out_ready")

        @block.tensor
        def _(pe):
            mm = nc.tensor.matmul
            tr = nc.tensor.transpose
            pe.wait_ge(sem("ident_ready"), 1)
            pe.wait_ge(sem("xs_ready"), NT + 1)
            for c in range(DC):
                if c >= 4:
                    pe.wait_ge(sem("nT_ready"), c - 3)
                for t in range(NT):
                    ins = tr(ps[:, c % 4, t * P:(t + 1) * P], xs[:, t, c * P:(c + 1) * P], ident[:])
                ins.then_inc(sem("xT_psum"), 1)
            for c in range(DC):
                ins = tr(ps[:, 4, c * META:(c + 1) * META], metax[0:META, c * P:(c + 1) * P], ident[0:META, 0:META])
            ins.then_inc(sem("xT_psum"), 1)
            pe.wait_ge(sem("nT_ready"), DC)
            pe.wait_ge(sem("nT_meta"), 1)
            n = 0
            for i in range(N_SHIFT):
                pe.wait_ge(slot_sem(i), landed[i])
                w = slot(i)
                for j in range(2):
                    if n >= 2:
                        pe.wait_ge(sem("chunk_out"), n - 1)
                    o = 2 * (n % 2)
                    for hf in range(2):
                        for c in range(DC):
                            ins = mm(ps[:, o + hf, 0:HALF], w[:, c, j * P:(j + 1) * P], nT[:, c, hf * HALF:(hf + 1) * HALF],
                                     start=(c == 0), stop=(c == DC - 1))
                    ins.then_inc(sem("chunk_psum"), 1)
                    n += 1
                pe.wait_ge(sem("chunk_psum"), n)
                pe.sem_inc(sem("piece_used"), 1)
            pe.wait_ge(sem("consts_ready"), 1)
            pe.sem_inc(sem("pe_phase"), 1)

            def qkv_products():
                for f, (i, kind, j, k) in enumerate(groups):
                    pe.wait_ge(slot_sem(i), landed[i])
                    if f >= 2:
                        pe.wait_ge(sem("fill_out"), f - 1)
                    w = slot(i)
                    b = 2 + f % 2
                    for c in range(DC):
                        if kind == "q":
                            ins = mm(ps[:, b, 0:HALF], w[:, c, (j % 2) * P:(j % 2 + 1) * P], nT[:, c, k * HALF:(k + 1) * HALF],
                                     start=(c == 0), stop=(c == DC - 1))
                        else:
                            nw = pieces[i][1][0][1]
                            k0, r = KT[k]
                            ins = mm(ps[0:r, b, 0:nw], nT[:, c, k0:k0 + r], w[:, c, 0:nw], start=(c == 0), stop=(c == DC - 1))
                        if c == DC - 1:
                            ins.then_inc(sem("fill_psum"), 1)
                        yield
            qkv_steps = qkv_products()

            def fill_qkv(count):
                for _ in range(count):
                    next(qkv_steps, None)

            pe.wait_ge(sem("dve_phase"), 1)
            pe.wait_ge(sem("act_phase"), 1)
            pe.wait_ge(sem("wd_ready"), 1)
            pe.wait_ge(sem("chunk_out"), SC)
            for c in range(RC):
                for q in range(2):
                    if c >= 1:
                        pe.wait_ge(sem("wa_used"), 2 * (c - 1) + q + 1)
                    rs = slice(64 * q, 64 * q + 64)
                    for hf in range(2):
                        ins = mm(ps[:, 6 * q + hf, 0:HALF], up_w[rs, c * P:(c + 1) * P], U[rs, 9, 1 + hf * HALF:1 + (hf + 1) * HALF], start=True, stop=True)
                    ins.then_inc(sem("wa_psum"), 1)
            fill_qkv(2 * DC)
            for c in range(RC):
                pe.wait_ge(sem("kk_sq"), c + 1)
                if c >= 1:
                    pe.wait_ge(sem("kk_used"), c)
                for hf in range(2):
                    ins = mm(ps[:, 4 + hf, 0:HALF], head_ones[:], Bt[:, c, hf * HALF:(hf + 1) * HALF], start=True, stop=True)
                ins.then_inc(sem("kk_psum"), 1)
            fill_qkv(8 * DC)
            pe.wait_ge(sem("kk_used"), RC)
            for c in range(RC):
                pe.wait_ge(sem("rk_ready"), c + 1)
                if c >= 1:
                    pe.wait_ge(sem("bonus_used"), c)
                for hf in range(2):
                    ins = mm(ps[:, 4 + hf, 0:HALF], head_ones[:], tb[:, c, hf * HALF:(hf + 1) * HALF], start=True, stop=True)
                ins.then_inc(sem("bonus_psum"), 1)
            fill_qkv((PREP - 10) * DC)
            pe.wait_ge(sem("bonus_used"), RC)
            pe.wait_ge(sem("tilde_ready"), 1)
            quads = [slice(0, 64), slice(64, 128)]

            def units(bank, lhs, rhs, acc=None, c0=0, c1=NCH):
                for c in range(c0, c1):
                    for q in quads:
                        ins = mm(psf[q, 512 * bank + c * CH:512 * bank + (c + 1) * CH], lhs(q, c), rhs(q, c), start=True, stop=True)
                return ins
            for p in range(RC):
                cm = lambda z: (lambda q, c: z[q, p, c * CH:(c + 1) * CH])
                um = lambda z: (lambda q, c: z[q, c, :])
                idq = lambda q, c: ident2[q, :]
                vsrc = lambda q, c: U[q, 6 + p, 1 + c * CH:1 + min((c + 1) * CH, L)]
                if p >= 1:
                    pe.wait_ge(sem("w1_ready"), p)
                    pe.wait_ge(sem("akv_ready"), p)
                for k, z in enumerate((At, Bt, Kt)):
                    if k == 1 and p >= 1:
                        pe.wait_ge(sem("y_out_rwkv"), NCH * p)
                    if k == 2:
                        pe.wait_ge(sem("tr_used"), 4 * p + 1)
                    units(6 * (k % 2), cm(z), idq).then_inc(sem("tr_psum"), 1)
                    if k == 1:
                        fill_qkv(2)
                pe.wait_ge(sem("tr_used"), 4 * p + 2)
                units(6, vsrc, idq, c1=NCH - 1)
                w = L - (NCH - 1) * CH
                for q in quads:
                    ins = mm(psf[q, 3072 + (NCH - 1) * CH:3072 + NCH * CH], At[q, p, LP - CH:LP], ident2[q, :], start=True, stop=True)
                for q in quads:
                    ins = mm(psf[q.start:q.start + w, 3072 + (NCH - 1) * CH:3072 + NCH * CH], vsrc(q, NCH - 1), ident2[q, :], start=True, stop=True)
                ins.then_inc(sem("tr_psum"), 1)
                fill_qkv(3)
                for k, (lhs, rhs) in enumerate(((Kt, At), (Kt, Rt), (Bt, At), (Bt, Rt), (At, Bt))):
                    if k >= 2:
                        pe.wait_ge(sem("g_used"), 5 * p + k - 1)
                    if k < 2 and p >= 1:
                        pe.wait_ge(sem("w2_ready"), p)
                        pe.wait_ge(sem("y_out_rwkv"), NCH * p)
                    if k == 1:
                        pe.wait_ge(sem("tr_used"), 4 * p + 4)
                    units(4 + 2 * (k % 2), cm(lhs), cm(rhs)).then_inc(sem("g_psum"), 1)
                    fill_qkv(1)
                pe.wait_ge(sem("g_used"), 5 * p + 5)
                pe.wait_ge(sem("tr_used"), 4 * p + 4)
                for lv in range(1, 6):
                    pe.wait_ge(sem("T_ready"), 6 * p + lv)
                    units(4, um(NTm), um(Tm)).then_inc(sem("H_psum"), 1)
                    fill_qkv(2)
                    pe.wait_ge(sem("H_ready"), 5 * p + lv)
                    if lv < 5:
                        units(6, um(TTm), um(Hm)).then_inc(sem("G_psum"), 1)
                    units(0, um(Hm), um(TTm)).then_inc(sem("G_psum"), 1)
                    fill_qkv(4)
                pe.wait_ge(sem("T_ready"), 6 * p + 6)
                units(0, um(AtT), um(TTm)).then_inc(sem("w1_psum"), 1)
                units(6, um(AKT), um(VT)).then_inc(sem("akv_psum"), 1)
                fill_qkv(2)
                pe.wait_ge(sem("akv_ready"), p + 1)
                units(4, um(TTm), um(Hm)).then_inc(sem("w2_psum"), 1)
                fill_qkv(3)
                if p == RC - 1:
                    fill_qkv(NF * DC)
                    pe.wait_ge(sem("fill_out"), NF)
                pe.wait_ge(sem("w1_ready"), p + 1)
                pe.wait_ge(sem("w2_ready"), p + 1)
                for c in range(NCH):
                    pe.wait_ge(sem("S_ready"), NCH * p + c + 1)
                    for q in quads:
                        ins = mm(ps[q, 6, 0:CH], W1T[q, c, :], Ssb[q, :], start=True, stop=True)
                    ins.then_inc(sem("u_psum"), 1)
                    if c >= 2:
                        pe.wait_ge(sem("y_out_rwkv"), NCH * p + c - 1)
                    yq = lambda q: ps[q, 5 + 2 * (c % 2), 0:CH]
                    for q in quads:
                        mm(yq(q), Ssb[q, :], Rt[q, p, c * CH:(c + 1) * CH], start=True, stop=False)
                        mm(yq(q), VT[q, c, :], RKT[q, c, :], start=False, stop=False)
                    pe.wait_ge(sem("U_ready"), NCH * p + c + 1)
                    if c < NCH - 1:
                        for q in quads:
                            mm(ps[q, 6, 128:128 + CH], KtT[q, c, :], VT[q, c, :], start=True, stop=False)
                            ins = mm(ps[q, 6, 128:128 + CH], BtT[q, c, :], Usb[q, :], start=False, stop=True)
                        ins.then_inc(sem("s_psum"), 1)
                    for q in quads:
                        ins = mm(yq(q), Usb[q, :], RBT[q, c, :], start=False, stop=True)
                    ins.then_inc(sem("y_psum"), 1)
                    fill_qkv(1)
                    if p == RC - 1 and 1 <= c <= 6:
                        pe.wait_ge(sem("fsq_ready"), c)
                        if c >= 2:
                            pe.wait_ge(sem("fms_ready"), c - 1)
                        for hf in range(2):
                            ins = mm(ps[:, 2 + hf, 0:HALF], head_ones[:], tmp_shift[:, 0, hf * HALF:(hf + 1) * HALF], start=True, stop=True)
                        ins.then_inc(sem("norm_psum"), 1)
            def gate_products():
                for n in range(3 * DC):
                    pe.wait_ge(sem(f"gate_w{n % 4}"), 16 * (n // 4 + 1))
                    if n >= 2:
                        pe.wait_ge(sem("gate_out"), n - 1)
                    for c in range(DC):
                        ins = mm(ps[:, 5 + 2 * (n % 2), :], gate_w[:, (n + 1) % 4, c, :], nT[:, c, META:L], start=(c == 0), stop=(c == DC - 1))
                        if c == DC - 1:
                            ins.then_inc(sem("gate_psum"), 1)
                        yield
            gate_steps = gate_products()

            def fill(count):
                for _ in range(count):
                    next(gate_steps, None)

            pe.wait_ge(sem("y_out_rwkv"), NCH * RC)
            fill(3)
            pe.wait_ge(sem("act_phase"), 2)
            for c in range(RC):
                if c >= 1:
                    pe.wait_ge(sem("ln_used"), c)
                for q, z in enumerate((yT[0], Rt)):
                    mm(ps[:, q, :], head_ones[:], z[:, c, 0:SEQ], start=True, stop=True).then_inc(sem("ln_psum"), 1)
                fill((5, DC)[c] if c < 2 else 0)
            pe.wait_ge(sem("ln_psum"), 2 * RC)
            pe.sem_inc(sem("pe_phase"), 1)
            fill((EARLY_GATES - 2) * DC)

            pe.wait_ge(sem("ln_used"), RC)
            pe.wait_ge(sem("f_ready"), 1)
            for hf in range(2):
                lo, hi = hf * HALF, (hf + 1) * HALF
                tiles = [(i, k0, r) for i, (k0, r) in enumerate(KT) if k0 < hi]
                for i, k0, r in tiles:
                    d0, d1 = max(lo, k0), min(hi, k0 + r)
                    first_ = i == 0
                    if first_ and lo == 0:
                        mm(ps[0:FH, hf, 0:P], flog[0:r, i, :], tri_le[0:r, 0:P], start=True, stop=False, skip_group_check=True)
                    elif d0 < d1:
                        mm(ps[0:FH, hf, d0 - lo:d1 - lo], flog[0:r, i, :], tri_le[0:r, d0 - k0:d1 - k0], start=False, stop=False, skip_group_check=True)
                    e0 = max(lo, k0 + r)
                    while e0 < hi:
                        e1 = min(hi, e0 + P)
                        ins = mm(ps[0:FH, hf, e0 - lo:e1 - lo], flog[0:r, i, :], ones[0:r, 0:e1 - e0],
                                 start=(i == 0 and e0 == lo), stop=False, skip_group_check=True)
                        e0 = e1
            ins = mm(ps[0:FH, 6, 0:1], ones[0:2, 0:FH], ones[0:2, 0:1], start=True, stop=True)
            ins.then_inc(sem("fcum_psum"), 1)
            pe.wait_ge(sem("fcum_ready"), 2)
            for hh in range(SH):
                cq, bq = qchunk("sb", hh, 0)
                ck, bk = qchunk("sb", hh, 1)
                q64 = slice(bq, bq + 64)
                if hh >= 1:
                    pe.wait_ge(sem("A_ready"), 5 * hh)
                for i, (k0, r) in enumerate(KT):
                    n = min(SEQ, L - k0)
                    ins = mm(ps[0:r, i, 0:n], QK[q64, ck, k0:k0 + r], QK[q64, cq, L - n:L], start=True, stop=False, skip_group_check=True)
                    ins.then_inc(sem("z_psum"), 1)
                fill(DC)
                pe.wait_ge(sem("sp_ready"), 5 * hh + 5)
                for i, (k0, r) in enumerate(KT):
                    n = min(SEQ, L - k0)
                    q0 = META if i == 0 else 0
                    mm(ps[0:r, i, 0:n], tri_sb[0:r, 0:r], s_b[i][0:r, 0:n], start=False, stop=False, skip_group_check=True)
                    for i2 in range(i + 1, 5):
                        k2, r2 = KT[i2]
                        n2_ = L - k2
                        mm(ps[0:r, i, n - n2_:n], neg_ones[0:r2, 0:r], s_b[i2][0:r2, 0:n2_], start=False, stop=False, skip_group_check=True)
                    w = r - q0
                    mm(ps[0:r, i, 0:w], ident[0:r, 0:r], neg_sb[0:r, q0:q0 + w], start=False, stop=True, skip_group_check=True).then_inc(sem("w_psum"), 1)
                fill(DC)
                row = 64 * (hh % 2) if hh < 4 else 0
                o = ps[row:row + 64, 6, :]
                for i, (k0, r) in enumerate(KT):
                    n = min(SEQ, L - k0)
                    pe.wait_ge(sem("A_ready"), 5 * hh + i + 1)
                    if i == 0 and hh >= 1:
                        pe.wait_ge(sem("sb_used"), hh)
                    ins = mm(o[:, SEQ - n:], V[0:r, i, hh * HD:(hh + 1) * HD], s_c[i][0:r, 0:n], start=(i == 0), stop=(i == 4), skip_group_check=True)
                ins.then_inc(sem("o_psum"), 1)
            pe.wait_ge(sem("o_psum"), SH)
            pe.sem_inc(sem("pe_phase"), 1)

            pe.wait_ge(sem("dve_phase"), 3)
            pe.wait_ge(sem("act_phase"), 3)
            pe.wait_ge(sem("frows"), 32 * FH)
            def scores(u):
                hh, i = u // NT, u % NT
                cq, bq = qchunk("fox", hh, 0)
                ck, _ = qchunk("fox", hh, 1)
                q64 = slice(bq, bq + 64)
                kn = META + P * (i + 1)
                qs = slice(META + i * P, META + (i + 1) * P)
                if u >= 2:
                    pe.wait_ge(sem("p_ready"), u - 1)
                for k0 in range(0, kn, 512):
                    k1 = min(kn, k0 + 512)
                    b = 2 * (u % 2) + k0 // 512
                    o = ps[:, b, 0:k1 - k0]
                    mm(o, QK[q64, cq, qs], QK[q64, ck, k0:k1], start=True, stop=False, skip_group_check=True)
                    mm(o, FL[0:2, hh, qs], FR[0:2, hh, k0:k1], start=False, stop=False, skip_group_check=True)
                    d0, d1 = max(k0, kn - P), k1
                    ins = mm(o[:, d0 - k0:d1 - k0], ident[:], neg_fox[:, d0 - (kn - P):d1 - (kn - P)], start=False, stop=True, skip_group_check=True)
                ins.then_inc(sem("s_ready"), 1)
            NU = FH * NT
            scores(0)
            for u in range(NU):
                hh, i = u // NT, u % NT
                if u + 1 < NU:
                    scores(u + 1)
                fill(FOX_FILL)
                pe.wait_ge(sem("pn_ready"), u + 1)
                if u >= 1:
                    pe.wait_ge(sem("pTs_ready"), u)
                for k in range(i + 1):
                    tr(ps[:, 4, k * P:(k + 1) * P], p_f[:, u % 2, k * P:(k + 1) * P], ident[:])
                tr(ps[0:16, 6, 256:256 + P], p_f[:, u % 2, (i + 1) * P:(i + 1) * P + 16], ident[:]).then_inc(sem("pT_psum"), 1)
                fill(FOX_FILL)
                pe.wait_ge(sem("pTs_ready"), u + 1)
                if u >= 1:
                    pe.wait_ge(sem("of_used"), u)
                row = 64 * (hh % 2) if hh < 4 else 64
                o = ps[row:row + 64, 6, 0:P]
                vs = slice(SW + hh * HD, SW + (hh + 1) * HD)
                for k in range(i + 1):
                    mm(o, V[:, k, vs], pT[:, u % 2, k, :], start=(k == 0), stop=False)
                mm(o, V[0:16, i + 1, vs], pT[0:16, u % 2, i + 1, :], start=False, stop=True).then_inc(sem("of_psum"), 1)
            pe.wait_ge(sem("of_psum"), NU)
            pe.sem_inc(sem("pe_phase"), 1)

            fill(8 * 3 * DC)
            n = 0
            for dc in range(DC):
                pe.wait_ge(sem(f"proj_w{dc % 2}"), 16 * 5 * (dc // 2 + 1))
                for b in range(3):
                    if n >= 2:
                        pe.wait_ge(sem("proj_used"), n - 1)
                    for c in range(3):
                        rs = slice(0, P) if b == 0 or c < 2 else slice(64 * (b - 1), 64 * b)
                        ins = mm(ps[:, 2 + n % 2, :], wpr[rs, dc % 2, 3 * b + c, :], yT[b][rs, c, :], start=(c == 0), stop=(c == 2))
                    ins.then_inc(sem("proj_psum"), 1)
                    n += 1
            pe.wait_ge(sem("merged_ready"), DC)
            pe.wait_ge(sem("wout_in"), 16)

            def second_norm_T(t):
                pe.wait_ge(sem("n2_ready"), t + 1)
                if t >= 2:
                    pe.wait_ge(sem("n2T_ready"), t - 1)
                b = 6 * (t % 2)
                for c in range(DC):
                    ins = tr(psf[:, 512 * b + c * P:512 * b + (c + 1) * P], n2[:, t, c * P:(c + 1) * P], ident[:])
                ins.then_inc(sem("n2T_psum"), 1)

            def router_logits(t):
                pe.wait_ge(sem("n2T_ready"), t + 1)
                for c in range(DC):
                    ins = mm(ps[:, 2, t * (NG + NE):(t + 1) * (NG + NE)], n2T[:, c, t * P:(t + 1) * P], rw[:, c, :], start=(c == 0), stop=(c == DC - 1))
                return ins
            for t in range(NT):
                for k in range(2):
                    if t >= 1:
                        pe.wait_ge(sem("wo_used"), 2 * (t - 1) + k + 1)
                    for c in range(DC):
                        ins = mm(ps[:, 4 + k, :], merged[:, c, t * P:(t + 1) * P], wout[:, c, k * 512:(k + 1) * 512], start=(c == 0), stop=(c == DC - 1))
                    ins.then_inc(sem("wo_psum"), 1)
                if t >= 1:
                    second_norm_T(t - 1)
                if t >= 2:
                    router_logits(t - 2)
            pe.wait_ge(sem("wo_psum"), 2 * NT)
            pe.sem_inc(sem("pe_phase"), 1)
            second_norm_T(NT - 1)
            router_logits(NT - 2)

            pe.wait_ge(sem("dve_phase"), 5)
            pe.wait_ge(sem("act_phase"), 5)
            router_logits(NT - 1).then_inc(sem("lg_psum"), 1)
            pe.wait_ge(sem("assign_ready"), 1)
            asg = rt[:, 12, :].rearrange("p (t e) -> p t e", t=NT)
            for t in range(NT):
                for t2 in range(t):
                    mm(ps[:, 3, t * NE:(t + 1) * NE], ones[:], asg[:, t2, :], start=(t2 == 0), stop=False)
                mm(ps[:, 3, t * NE:(t + 1) * NE], tri_lt[:], asg[:, t, :], start=(t == 0), stop=True)
            for t in range(NT):
                ins = mm(ps[:, 3, NT * NE:(NT + 1) * NE], ones[:], asg[:, t, :], start=(t == 0), stop=(t == NT - 1))
            ins.then_inc(sem("rank_psum"), 1)

            def index(t):
                for k in range(NT):
                    ins = mm(ps[:, 7, 0:1], Pm[:, k, :], tokid[:, k:k + 1], start=(k == 0), stop=(k == NT - 1))
                ins.then_inc(sem("idx_psum"), 1)

            def rows_T(t, s, landed_):
                pe.wait_ge(sem(f"xg_in{s}"), landed_)
                for k in range(2):
                    for c in range(4):
                        ins = tr(ps[:, k, c * P:(c + 1) * P], xg[:, s, (4 * k + c) * P:(4 * k + c + 1) * P], ident[:])
                    ins.then_inc(sem("xgT_psum"), 1)

            def gate_up(t, s, bank, landed_):
                pe.wait_ge(sem("xgT_ready"), t * 2 + 2)
                pe.wait_ge(sem(f"moe_w{s}"), landed_)
                for c in range(DC):
                    ins = mm(ps[:, bank, :], xgT[:, s, c, :], w1[:, s, c, :], start=(c == 0), stop=(c == DC - 1))
                ins.then_inc(sem("gu_psum"), 1)

            def hidden_T(t, s):
                pe.wait_ge(sem("hg_ready"), t + 1)
                for c in range(2):
                    ins = tr(ps[:, 3, c * P:(c + 1) * P], hg[:, s, c * P:(c + 1) * P], ident[:])
                ins.then_inc(sem("hT_psum"), 1)

            def down(t, s, landed_):
                pe.wait_ge(sem("hT_ready"), t + 1)
                pe.wait_ge(sem(f"moe_d{s}"), landed_)
                for k in range(2):
                    for c in range(2):
                        ins = mm(ps[:, 4 + k, :], hT[:, s, c, :], w2[:, s, c, 512 * k:512 * k + 512], start=(c == 0), stop=(c == 1))
                ins.then_inc(sem("down_psum"), 1)

            pe.wait_ge(sem("pm_ready"), 1)
            index(0)
            pe.wait_ge(sem("pm_ready"), 2)
            pe.wait_ge(sem("idx_ready"), 1)
            index(1)
            rows_T(0, 0, 16)
            for t in range(NE + 1):
                if t < NE:
                    if t >= 2:
                        pe.wait_ge(sem("hg_ready"), t - 1)
                    gate_up(t, t % 2, 2 + 4 * (t % 2), 32 * (t // 2 + 1))
                if t >= 1:
                    if t >= 2:
                        pe.wait_ge(sem("hT_ready"), t - 1)
                    hidden_T(t - 1, (t - 1) % 2)
                if t + 1 < NE:
                    pe.wait_ge(sem("xgT_ready"), 2 * t + 2)
                    rows_T(t + 1, (t + 1) % 2, 16 * ((t + 1) // 2 + 1))
                if t + 2 < NE:
                    pe.wait_ge(sem("pm_ready"), t + 3)
                    pe.wait_ge(sem("idx_ready"), t + 2)
                    index(t + 2)
                if t >= 1:
                    if t >= 2:
                        pe.wait_ge(sem("y_low"), t - 1)
                        pe.wait_ge(sem("y_high"), t - 1)
                    down(t - 1, (t - 1) % 2, 16 * ((t - 1) // 2 + 1))
            pe.wait_ge(sem("ov_ready"), 1)
            n_ov = pe.value_load(ovi[0:1, 0:1], min_val=0, max_val=NOV)
            with pe.Fori(0, NOV) as k:
                with pe.If(k < n_ov):
                    t = k + NE
                    pe.wait_ge(sem("pm_ready"), k + NE + 1)
                    pe.wait_ge(sem("y_low"), k + NE)
                    pe.wait_ge(sem("y_high"), k + NE)
                    index(t)
                    rows_T(t, 0, k * 16 + 16 * (NE // 2 + 1))
                    gate_up(t, 0, 2, k * 32 + 32 * (NE // 2 + 1))
                    hidden_T(t, 0)
                    down(t, 0, k * 16 + 16 * (NE // 2 + 1))


_INS = ["x", "meta_tokens", "norm1_g", "w_in", "rwkv_mu", "rwkv_w_up", "rwkv_w0", "rwkv_a_up", "rwkv_a0",
        "rwkv_k_k", "rwkv_k_a", "rwkv_r_k", "rwkv_ln_g", "rwkv_ln_b", "fox_f_b", "fox_q_g", "fox_k_g",
        "w_p_rwkv", "w_p_sb", "w_p_fox", "w_out", "norm2_g", "moe_wg", "moe_bg", "moe_we", "moe_be",
        "moe_w_gate", "moe_w_up", "moe_w_down"]


def kernel(**inputs):
    import numpy as _np
    import concourse.bacc as _bacc
    from concourse import mybir as _mybir
    from concourse.bass_utils import run_bass_kernel_spmd as _run

    nc = _bacc.Bacc("TRN2", target_bir_lowering=False, num_devices=1)
    arrays, args = {}, []
    for name in _INS:
        a = _np.ascontiguousarray(inputs[name])
        if name != "meta_tokens":
            a = a[0]
        arrays["in_" + name] = a
        args.append(nc.dram_tensor("in_" + name, a.shape, _mybir.dt.from_np(a.dtype), kind="ExternalInput").ap())
    o = nc.dram_tensor("out_0", (SEQ, D), _mybir.dt.float32, kind="ExternalOutput").ap()
    hybrid_layer(nc, *args, o)
    r = _run(nc, [arrays], core_ids=[0])
    return r.results[0]["out_0"].reshape(1, SEQ, D)
```
